# Optimizing a Trainium2 kernel written in Bass

```python
import math
import jax, jax.numpy as jnp
from jax import lax
import numpy as np

D_MODEL = 2048
BATCH = 1
SEQ = 256
DEPTH = 2

N_EVEN = (DEPTH + 1) // 2
N_ODD = DEPTH // 2
RMS_EPS = 1e-6

HG_HEADS = 8
HG_KDIM = 128
HG_VDIM = D_MODEL // 2 // HG_HEADS
HG_CHUNK = 64
HG_K_TOTAL = HG_HEADS * HG_KDIM
HG_V_TOTAL = HG_HEADS * HG_VDIM

SB_HEADS = 8
SB_HEAD_DIM = D_MODEL // 2 // SB_HEADS
SB_BLOCK = 128
SB_TOTAL = SB_HEADS * SB_HEAD_DIM

AB_SIZES = (HG_K_TOTAL, HG_K_TOTAL, HG_V_TOTAL, HG_V_TOTAL, SB_TOTAL, SB_TOTAL, SB_TOTAL)
AB_IN_DIM = sum(AB_SIZES)
AB_SPLITS = tuple(int(v) for v in np.cumsum(AB_SIZES)[:-1])
MIX_WIDTH = HG_V_TOTAL + SB_TOTAL

POOL_WINDOWS = (2, 4, 8, 16)
N_POOL_GROUPS = len(POOL_WINDOWS)
POOL_GROUP = D_MODEL // N_POOL_GROUPS

FFN_HIDDEN = -(-8 * D_MODEL // (3 * 256)) * 256

kernel_name = 'hgrn2_stickbreak_pool_hybrid'

def rms_norm(x, gain):
    x32 = x.astype(jnp.float32)
    y = x32 * lax.rsqrt(jnp.mean(x32 * x32, axis=-1, keepdims=True) + RMS_EPS)
    return (y * gain.astype(jnp.float32)).astype(x.dtype)

def swiglu(h, w_gate, w_up, w_down):
    return (jax.nn.silu(h @ w_gate) * (h @ w_up)) @ w_down

def hgrn2_chunked(q, log_f, k, v):
    b, s, h, dk = q.shape
    dv = v.shape[-1]
    nc = s // HG_CHUNK

    def to_chunks(t):
        return t.reshape(b, nc, HG_CHUNK, h, t.shape[-1]).transpose(1, 0, 3, 2, 4)

    causal = jnp.tril(jnp.ones((HG_CHUNK, HG_CHUNK), dtype=bool))

    def step(state, inp):
        qc, gc, kc, vc = inp
        g_cum = jnp.cumsum(gc, axis=-2)
        o_inter = jnp.einsum('bhtk,bhkv->bhtv', qc * jnp.exp(g_cum), state)
        diff = g_cum[:, :, :, None, :] - g_cum[:, :, None, :, :]
        decay = jnp.exp(jnp.where(causal[:, :, None], diff, -jnp.inf))
        att = jnp.einsum('bhtk,bhtsk,bhsk->bhts', qc, decay, kc)
        o_intra = jnp.einsum('bhts,bhsv->bhtv', att, vc)
        g_last = g_cum[:, :, -1:, :]
        new_state = (jnp.exp(g_last[:, :, 0, :])[..., None] * state
                     + jnp.einsum('bhsk,bhsv->bhkv', kc * jnp.exp(g_last - g_cum), vc))
        return new_state, o_inter + o_intra

    s0 = jnp.zeros((b, h, dk, dv), jnp.float32)
    _, o = lax.scan(step, s0, (to_chunks(q), to_chunks(log_f), to_chunks(k), to_chunks(v)))
    return o.transpose(1, 0, 3, 2, 4).reshape(b, s, h, dv)

def stick_breaking_attention(q, k, v):
    b, h, s, d = q.shape
    nb = s // SB_BLOCK
    scale = 1.0 / math.sqrt(d)
    q_blocks = q.reshape(b, h, nb, SB_BLOCK, d).transpose(2, 0, 1, 3, 4)
    key_pos = jnp.arange(s)

    def block(args):
        qb, start = args
        z = jnp.einsum('bhqd,bhsd->bhqs', qb, k).astype(jnp.float32) * scale
        query_pos = start + jnp.arange(SB_BLOCK)
        mask = key_pos[None, :] < query_pos[:, None]
        log_keep = jnp.where(mask, jax.nn.log_sigmoid(-z), 0.0)
        later = lax.cumsum(log_keep, axis=3, reverse=True) - log_keep
        weights = jnp.where(mask, jnp.exp(jax.nn.log_sigmoid(z) + later), 0.0)
        return jnp.einsum('bhqs,bhsd->bhqd', weights.astype(v.dtype), v)

    starts = jnp.arange(nb, dtype=jnp.int32) * SB_BLOCK
    o = lax.map(block, (q_blocks, starts))
    return o.transpose(1, 2, 0, 3, 4).reshape(b, h, s, d)

def hybrid_ab_mixer(h, w_in, lower_bound, hg_out_norm, w_out):
    b, s, _ = h.shape
    proj = h @ w_in
    qa, fa, ia, ga, qb, kb, vb = jnp.split(proj, AB_SPLITS, axis=-1)

    f = lower_bound + (1.0 - lower_bound) * jax.nn.sigmoid(fa.astype(jnp.float32))
    heads_k = lambda t: t.reshape(b, s, HG_HEADS, HG_KDIM)
    o_a = hgrn2_chunked(heads_k(jax.nn.silu(qa.astype(jnp.float32))),
                        heads_k(jnp.log(f)),
                        heads_k(1.0 - f),
                        ia.astype(jnp.float32).reshape(b, s, HG_HEADS, HG_VDIM))
    o_a = rms_norm(o_a, hg_out_norm) * jax.nn.silu(ga.astype(jnp.float32)).reshape(b, s, HG_HEADS, HG_VDIM)
    o_a = o_a.reshape(b, s, HG_V_TOTAL).astype(h.dtype)

    heads_b = lambda t: t.reshape(b, s, SB_HEADS, SB_HEAD_DIM).transpose(0, 2, 1, 3)
    o_b = stick_breaking_attention(heads_b(qb), heads_b(kb), heads_b(vb))
    o_b = o_b.transpose(0, 2, 1, 3).reshape(b, s, SB_TOTAL).astype(h.dtype)

    return jnp.concatenate([o_a, o_b], axis=-1) @ w_out

def multiscale_pool_mixer(h, w_groups, scale):
    b, s, d = h.shape
    hg = h.astype(jnp.float32).reshape(b, s, N_POOL_GROUPS, POOL_GROUP)
    prefix = jnp.concatenate([jnp.zeros((b, 1, N_POOL_GROUPS, POOL_GROUP), jnp.float32),
                              jnp.cumsum(hg, axis=1)], axis=1)
    pos = jnp.arange(s)
    outs = []
    for gi, w in enumerate(POOL_WINDOWS):
        lo = jnp.maximum(pos + 1 - w, 0)
        window_sum = prefix[:, 1:, gi] - prefix[:, lo, gi]
        count = jnp.minimum(pos + 1, w).astype(jnp.float32)
        outs.append(window_sum / count[None, :, None] - hg[:, :, gi])
    pooled = jnp.stack(outs, axis=2).astype(h.dtype)
    mixed = jnp.einsum('bsgc,gcd->bsgd', pooled, w_groups)
    return mixed.reshape(b, s, d) * scale

def setup_inputs(seed: int = 0) -> dict:
    key = jax.random.key(seed)
    ks = jax.random.split(key, 14)
    f32 = jnp.float32
    nrm = lambda k, shape, fan_in: jax.random.normal(k, shape, f32) * (fan_in ** -0.5)
    return {
        'x': jax.random.normal(ks[0], (BATCH, SEQ, D_MODEL), f32),
        'mix_norm': 1.0 + 0.02 * jax.random.normal(ks[1], (DEPTH, D_MODEL), f32),
        'ffn_norm': 1.0 + 0.02 * jax.random.normal(ks[2], (DEPTH, D_MODEL), f32),
        'final_norm': 1.0 + 0.02 * jax.random.normal(ks[3], (D_MODEL,), f32),
        'ab_w_in': nrm(ks[4], (N_EVEN, D_MODEL, AB_IN_DIM), D_MODEL),
        'lb_logits': 0.1 * jax.random.normal(ks[5], (N_EVEN + 1, HG_K_TOTAL), f32),
        'hg_out_norm': 1.0 + 0.02 * jax.random.normal(ks[6], (N_EVEN, HG_VDIM), f32),
        'ab_w_out': nrm(ks[7], (N_EVEN, MIX_WIDTH, D_MODEL), MIX_WIDTH),
        'pool_w': nrm(ks[8], (N_ODD, N_POOL_GROUPS, POOL_GROUP, POOL_GROUP), POOL_GROUP),
        'pool_scale': 1.0 + 0.02 * jax.random.normal(ks[9], (N_ODD, D_MODEL), f32),
        'ffn_w_gate': nrm(ks[10], (DEPTH, D_MODEL, FFN_HIDDEN), D_MODEL),
        'ffn_w_up': nrm(ks[11], (DEPTH, D_MODEL, FFN_HIDDEN), D_MODEL),
        'ffn_w_down': nrm(ks[12], (DEPTH, FFN_HIDDEN, D_MODEL), FFN_HIDDEN),
    }

def reference(x, mix_norm, ffn_norm, final_norm, ab_w_in, lb_logits, hg_out_norm, ab_w_out,
              pool_w, pool_scale, ffn_w_gate, ffn_w_up, ffn_w_down):
    lower_bounds = jnp.cumsum(jax.nn.softmax(lb_logits.astype(jnp.float32), axis=0), axis=0)
    for layer in range(DEPTH):
        h = rms_norm(x, mix_norm[layer])
        i = layer // 2
        if layer % 2 == 0:
            mix = hybrid_ab_mixer(h, ab_w_in[i], lower_bounds[i], hg_out_norm[i], ab_w_out[i])
        else:
            mix = multiscale_pool_mixer(h, pool_w[i], pool_scale[i])
        x = x + mix.astype(x.dtype)
        h = rms_norm(x, ffn_norm[layer])
        x = x + swiglu(h, ffn_w_gate[layer], ffn_w_up[layer], ffn_w_down[layer]).astype(x.dtype)
    return rms_norm(x, final_norm)


_drawn_inputs = setup_inputs


def setup_inputs(seed=0):
    import zlib

    import numpy as np

    out = dict(_drawn_inputs(seed))
    spreads = {}
    factors = {'mix_norm': 2.741,
     'ffn_norm': 3.272,
     'final_norm': 2.939,
     'lb_logits': 8.0,
     'hg_out_norm': 6.301,
     'pool_scale': 4.78}
    for name, (base, spread) in spreads.items():
        noise = np.random.default_rng([zlib.crc32(name.encode()), seed]).standard_normal(out[name].shape)
        drawn = base * np.exp(spread * noise) if base else spread * noise
        out[name] = __import__('jax').numpy.asarray(drawn.astype(out[name].dtype))
    for name, factor in factors.items():
        out[name] = (out[name] * factor).astype(out[name].dtype)
    return out
```

```python
from contextlib import ExitStack, contextmanager

import concourse.bass as bass
from concourse import mybir

F32 = mybir.dt.float32
F32R = mybir.dt.float32r
U32 = mybir.dt.uint32
ALU = mybir.AluOpType
ACT = mybir.ActivationFunctionType

P = 128
TOKENS = 256
D = 2048
DT = D // P
FFN = 5632
HEADS = 8
PAIRS = HEADS // 2
EPS = 1e-6
RING = 4
COLS = 256
DEPTH = 8
SLOT = DEPTH * COLS
QA, FA, IA, GA, QB, KB, VB = (1024 * n for n in range(7))
UNITS = (8, 8, 6)
WINDOWS = (2, 4, 8, 16)
POOL_OUT = (1, 2, 1, 2)
HG_LINKS = 29
LEVELS = 7

SB_SLOTS, SB_JOBS = 6, 3
HG_SLOTS, HG_JOBS = 8, 4
S_HG, J_HG = SB_SLOTS * PAIRS, SB_JOBS * PAIRS
S_OUTB, J_OUTB = S_HG + HG_SLOTS * PAIRS, J_HG + HG_JOBS * PAIRS
S_OUTA, J_OUTA = S_OUTB + 8, J_OUTB + 8
FFN_SLOTS = 4 * sum(UNITS) + 16 * len(UNITS)
FFN_JOBS = 2 * sum(UNITS) + 8 * len(UNITS)
S_FFN0, J_FFN0 = S_OUTA + 8, J_OUTA + 8
S_POOL, J_POOL = S_FFN0 + FFN_SLOTS, J_FFN0 + FFN_JOBS
S_FFN1, J_FFN1 = S_POOL + 8, J_POOL + 8
SLOTS = S_FFN1 + FFN_SLOTS
C_FFN = J_OUTB

V_MIX, V_FFN, V_FINAL, V_SCALE, V_LB, V_HGN, V_ALL = 0, 32, 64, 80, 96, 112, 113


def ffn_groups(s0, j0):
    out, u = [], 0
    for n in UNITS:
        out.append((s0, j0, u, n))
        s0, j0, u = s0 + 4 * n + 16, j0 + 2 * n + 8, u + n
    return out


class Count:

    def __init__(self, base, stride=0, i=0):
        self.base, self.stride, self.i = base, stride, i

    def __add__(self, k):
        return Count(self.base + k, self.stride, self.i)

    def times(self, k):
        return Count(self.base * k, self.stride * k, self.i)

    def lap(self):
        return Count(self.base // RING, self.stride // RING, self.i)

    @property
    def place(self):
        assert self.stride % RING == 0
        return self.base % RING

    @property
    def parity(self):
        assert self.stride % 2 == 0
        return self.base % 2

    @property
    def value(self):
        return self.base + self.i * self.stride if self.stride else self.base


def need(eng, semaphore, count):
    v = count.value if isinstance(count, Count) else count
    if not (isinstance(v, int) and v <= 0):
        eng.wait_ge(semaphore, v)


class Chain:

    def __init__(self, eng, sem):
        self.eng, self.sem, self.base, self.n, self.used = eng, sem, 0, 0, 0

    def link(self, ins):
        ins.then_inc(self.sem, 1)
        self.n += 1

    def settle(self):
        self.eng.wait_ge(self.sem, self.base + self.n)

    @contextmanager
    def loop(self, first, end, per):
        start = self.base + self.n
        with self.eng.Fori(first, end) as i:
            self.base, self.n = i * per + (start - first * per), 0
            yield i
            assert self.n == per, f"{self.n} links in a loop's body"
        self.base, self.n = start + (end - first) * per, 0


def one(tile):
    v = tile.value if isinstance(tile, Count) else tile
    return slice(v, v + 1) if isinstance(v, int) else bass.ds(v, 1)


def both(tile):
    v = tile.value
    return slice(v, v + 2) if isinstance(v, int) else bass.ds(v, 2)


def tiles_of(p):
    return both(p.times(2))


def trunk(nc, x, mix_norm, ffn_norm, final_norm, ab_w_in, lb_logits, hg_out_norm, ab_w_out,
          pool_w, pool_scale, w_gate, w_up, w_down, out):
    with ExitStack() as ctx:
        def sb(name, shape, dt=F32):
            return ctx.enter_context(nc.sbuf_tensor(name, shape, dt))

        def sem(name):
            return ctx.enter_context(nc.semaphore(name))

        def semaphores(name, n):
            return [sem(f"{name}{i}") for i in range(n)]

        raw = sb("raw", [P, RING, SLOT])
        hi = sb("hi", [P, RING, SLOT], F32R)
        lo = sb("lo", [P, RING, SLOT], F32R)
        xT = sb("xT", [P, DT, TOKENS])
        act = sb("act", [P, DT, 2, TOKENS], F32R)
        mid = sb("mid", [P, DT, 2, TOKENS], F32R)
        ident = sb("ident", [P, P])
        ones = sb("ones", [P, P])
        vecs = sb("vecs", [P, V_ALL])
        vrows = sb("vrows", [P, P])
        lbs = sb("lbs", [P, 2, HEADS])
        eps = sb("eps", [P, 1])
        rows = sb("rows", [P, 2])
        inv = sb("inv", [P, 16])
        rstd = sb("rstd", [P, TOKENS])
        cross = sb("cross", [P, 2, TOKENS])
        tri = sb("tri", [P, 2, P])
        lmask = sb("lmask", [P, LEVELS, 64])
        work = sb("work", [P, 5904])

        def pair(a):
            return work[:, a:a + 512].rearrange("p (c t) -> p c t", c=2)

        q, k, vT = pair(0), pair(512), pair(1024)
        h_tmp = [pair(4096), pair(4608)]
        xg = [pair(5120), cross[:]]
        vnat = work[:, 1536:2048].rearrange("p (h s v) -> p h s v", h=2, s=2)
        att = work[:, 2048:2816].rearrange("p (h b t) -> p h b t", h=2, b=3)
        att_sb = work[:, 2048:2816].rearrange("p (h t) -> p h t", h=2)
        att_own = work[:, 2048:2560].rearrange("p (g t) -> p g t", g=4)
        att_cross = work[:, 2560:2816].rearrange("p (h t) -> p h t", h=2)
        W2 = 386
        sg = work[:, 2816:2816 + 772]
        kp = work[:, 3588:3588 + 772]
        cum = work[:, 4360:4360 + 772]
        reset = work[:, 5132:5132 + 772]
        sg2, kp2, reset2 = (a.rearrange("p (h w) -> p h w", h=2) for a in (sg, kp, reset))
        pre, suf, gate = pair(2816), pair(3328), pair(4864)
        xl = [pair(3840), pair(4352)]
        tgate, sig, tup = pair(0), pair(512), pair(1024)
        acc, sq = pair(4096), pair(4608)
        pb = [work[:, 1088 * n:1088 * (n + 1)].rearrange("p (c t) -> p c t", c=4) for n in range(3)]
        stage = work[:, 0:4096].rearrange("p (h d) -> p h d", h=2)
        diag = work[:, 5120:5376].rearrange("p (h t) -> p h t", h=2)

        main = ctx.enter_context(nc.psum_tensor("main", [P, 4, 512], F32))
        aux = ctx.enter_context(nc.psum_tensor("aux", [P, 4, 512], F32))

        def bank(job):
            return main[:, 2 * job.parity:2 * job.parity + 2, :]

        x_loaded, raw_loaded = semaphores("x_loaded", 2), semaphores("raw_loaded", RING)
        out_scaled = semaphores("out_scaled", 2)
        ident_made = sem("ident_made")
        pads_made = sem("pads_made")
        sumsq = sem("sumsq")
        hi_ready = sem("hi_ready")
        cross_ready = sem("cross_ready")
        row_sq = sem("row_sq")
        row_rms = sem("row_rms")
        vec_T = sem("vec_T")
        vecs_ready = sem("vecs_ready")
        lb_diff = sem("lb_diff")
        lb_ready = sem("lb_ready")
        h_hi = sem("h_hi")
        wt_ready = sem("wt_ready")
        vnat_ready = sem("vnat_ready")
        sb_hi = sem("sb_hi")
        sb_sig = sem("sb_sig")
        f_sig = sem("f_sig")
        q_sig = sem("q_sig")
        g_sig = sem("g_sig")
        cross_att = sem("cross_att")
        hg_sq = sem("hg_sq")
        hg_rms = sem("hg_rms")
        hg_hi = sem("hg_hi")
        g_hi = sem("g_hi")
        sq_ready = sem("sq_ready")
        q_ready = sem("q_ready")
        next_hi = sem("next_hi")
        t_sig = sem("t_sig")
        rms_done = sem("rms_done")
        pool_hi = sem("pool_hi")
        lo_ready = sem("lo_ready")
        job_emptied = sem("job_emptied")
        next_ready = sem("next_ready")
        x_copied = sem("x_copied")
        row_rstd = sem("row_rstd")
        diag_ready = sem("diag_ready")
        g_ready = sem("g_ready")
        rstd_bc = sem("rstd_bc")
        h_made = sem("h_made")
        h_ready = sem("h_ready")
        sb_out = sem("sb_out")
        w_ready = sem("w_ready")
        x_level = sem("x_level")
        level_kept = sem("level_kept")
        f_ready = sem("f_ready")
        hg_o = sem("hg_o")
        hg_out = sem("hg_out")
        t_scaled = sem("t_scaled")
        u_made = sem("u_made")
        hidden = sem("hidden")
        pooled = sem("pooled")
        pool_ready = sem("pool_ready")
        xg_ready = sem("xg_ready")
        slot_used = sem("slot_used")
        x_T = sem("x_T")
        v_T = sem("v_T")
        w_T = sem("w_T")
        sb_pv = sem("sb_pv")
        z_done = sem("z_done")
        level_done = sem("level_done")
        diag_done = sem("diag_done")
        hg_pv = sem("hg_pv")
        hg_mean = sem("hg_mean")
        mean_done = sem("mean_done")
        o_T = sem("o_T")
        out_stored = sem("out_stored")
        dve_chain = sem("dve_chain")
        o_copied = sem("o_copied")
        vec_loaded = sem("vec_loaded")
        pool_chain = sem("pool_chain")
        block = ctx.enter_context(nc.Block())

        @block.sync
        def _(sp):
            rows_of = [(mix_norm.rearrange("l (t p) -> (l t) p", p=P), V_MIX, 32),
                       (ffn_norm.rearrange("l (t p) -> (l t) p", p=P), V_FFN, 32),
                       (final_norm.rearrange("(t p) -> t p", p=P), V_FINAL, 16),
                       (pool_scale.rearrange("l (t p) -> (l t) p", p=P), V_SCALE, 16),
                       (lb_logits.rearrange("l (t p) -> (l t) p", p=P), V_LB, 16),
                       (hg_out_norm, V_HGN, 1)]
            for src, at, n in rows_of:
                sp.dma_start(vrows[at:at + n, :], src).then_inc(vec_loaded, 16)
            for h in range(2):
                sp.dma_start(stage[:, h, :], x[0, h * P:(h + 1) * P, :]).then_inc(x_loaded[h], 16)

            def load(s, src, depth):
                need(sp, lo_ready, s + (1 - RING))
                dst = raw[:, s.place, 0:depth * COLS].rearrange("p (k c) -> p k c", k=depth)
                sp.dma_start(dst, src).then_inc(raw_loaded[s.place], 16)

            def block_rows(w, row, depth, col):
                return w[row:row + depth * P, bass.ds(col, COLS)].rearrange("(k p) c -> p k c", p=P)

            for p in range(PAIRS):
                for n, part in enumerate((QB, KB, VB)):
                    for half in range(2):
                        load(Count(SB_SLOTS * p + 2 * n + half),
                             block_rows(ab_w_in[0], 1024 * half, DEPTH, part + COLS * p), DEPTH)
            with sp.Fori(1, PAIRS + 1) as p:
                for n, part in enumerate((FA, QA, IA, GA)):
                    for half in range(2):
                        load(Count(S_HG + 2 * n + half - HG_SLOTS, HG_SLOTS, p),
                             block_rows(ab_w_in[0], 1024 * half, DEPTH, p * COLS + (part - COLS)), DEPTH)
            for s0, row in ((S_OUTB, 1024), (S_OUTA, 0)):
                with sp.Fori(1, 3) as i:
                    for j in range(4):
                        load(Count(s0 + j - 4, 4, i),
                             block_rows(ab_w_out[0], row, DEPTH, i * (4 * COLS) + (j - 4) * COLS), DEPTH)
            for layer, s_ffn in enumerate((S_FFN0, S_FFN1)):
                if layer == 1:
                    for j in range(8):
                        src = pool_w[0, j // 2, :, COLS * (j % 2):COLS * (j % 2 + 1)].rearrange("(k p) c -> p k c", p=P)
                        load(Count(S_POOL + j), src, 4)
                for s0, j0, u0, n in ffn_groups(s_ffn, 0):
                    with sp.Fori(1, n + 1) as i:
                        for m, w in enumerate((w_gate, w_up)):
                            for half in range(2):
                                load(Count(s0 + 2 * m + half - 4, 4, i),
                                     block_rows(w[layer], 1024 * half, DEPTH, i * COLS + (u0 - 1) * COLS), DEPTH)
                    with sp.Fori(1, 5) as i:
                        for j in range(4):
                            load(Count(s0 + 4 * n + j - 4, 4, i),
                                 block_rows(w_down[layer], (2 * u0 + n * (j % 2)) * P, n,
                                            i * (2 * COLS) + (j // 2 - 2) * COLS), n)
            for c in range(2):
                for h in range(2):
                    sp.wait_ge(out_scaled[h], c + 1)
                    sp.dma_start(out[0, h * P:(h + 1) * P, c * 1024:(c + 1) * 1024],
                                 stage[:, h, c * 1024:(c + 1) * 1024]).then_inc(out_stored, 16)
            sp.wait_ge(out_stored, 4 * 16)

        @block.gpsimd
        def _(pool):
            chain = Chain(pool, pool_chain)
            chain.link(nc.gpsimd.memset(ident[:], 0.0))
            chain.link(nc.gpsimd.memset(ones[:], 1.0))
            chain.link(nc.gpsimd.memset(tri[:], 1.0))
            chain.link(nc.gpsimd.memset(lmask[:], 1.0))
            chain.link(nc.gpsimd.memset(eps[:], EPS))
            for t in range(16):
                chain.link(nc.gpsimd.memset(inv[:, t:t + 1], 1.0 / (t + 1)))
            chain.settle()
            nc.gpsimd.affine_select(out=ident[:], in_=ident[:], compare_op=ALU.not_equal, fill=1.0, base=0,
                                    pattern=[[-1, P]], channel_multiplier=1).then_inc(ident_made, 1)
            chain.link(nc.gpsimd.affine_select(out=tri[:, 0, :], in_=tri[:, 0, :], compare_op=ALU.is_gt, fill=0.0,
                                               base=0, pattern=[[-1, P]], channel_multiplier=1))
            chain.link(nc.gpsimd.affine_select(out=tri[:, 1, :], in_=tri[:, 1, :], compare_op=ALU.is_ge, fill=0.0,
                                               base=0, pattern=[[1, P]], channel_multiplier=-1))
            for lv in range(LEVELS):
                h = 1 << lv
                m = lmask[:, lv, :].rearrange("p (n j) -> p n j", j=h)
                chain.link(nc.gpsimd.affine_select(out=m, in_=m, compare_op=ALU.is_ge, fill=0.0, base=0,
                                                   pattern=[[-2 * h, 64 // h], [0, h]], channel_multiplier=1))
            chain.settle()
            for lv in range(LEVELS):
                h = 1 << lv
                m = lmask[:, lv, :].rearrange("p (n j) -> p n j", j=h)
                chain.link(nc.gpsimd.affine_select(out=m, in_=m, compare_op=ALU.is_ge, fill=0.0, base=h - 1,
                                                   pattern=[[2 * h, 64 // h], [0, h]], channel_multiplier=-1))

            pool.wait_ge(h_ready, 8)
            chain.link(nc.gpsimd.memset(sg, 0.0))
            chain.link(nc.gpsimd.memset(kp, 0.0))
            chain.link(nc.gpsimd.memset(reset, 0.0))
            chain.settle()
            chain.link(nc.gpsimd.memset(reset2[:, :, P:P + 1], 1.0))
            nc.gpsimd.memset(reset2[:, :, W2 - 1:W2], 1.0).then_inc(pads_made, 1)

            for n in range(4):
                if n == 0:
                    pool.wait_ge(hg_out, PAIRS)
                else:
                    pool.wait_ge(mean_done, n)
                nc.gpsimd.memset(acc, 0.0).then_inc(sumsq, 1)
                with pool.Fori(0, 8) as i:
                    pool.wait_ge(sq_ready, i + (8 * n + 1))
                    pool.wait_ge(sumsq, i + (9 * n + 1))
                    nc.gpsimd.tensor_tensor(acc, acc, sq, ALU.add).then_inc(sumsq, 1)

        @block.scalar
        def _(sc):
            def copy(out_, in_):
                return nc.scalar.copy(out_, in_)

            def split(s):
                need(sc, raw_loaded[s.place], (s.lap() + 1).times(16))
                need(sc, slot_used, s + (1 - RING))
                copy(hi[:, s.place, :], raw[:, s.place, :]).then_inc(hi_ready, 1)

            def take_cross(s, job):
                need(sc, slot_used, s + 1)
                need(sc, job_emptied, job)
                copy(cross[:], bank(job)[:, :, TOKENS:]).then_inc(cross_ready, 1)

            def sigmoid(out_, in_, scale=1.0):
                return nc.scalar.activation(out_, in_, ACT.Sigmoid, scale=scale)

            def root(out_, in_, scale):
                return nc.scalar.activation(out_, in_, ACT.Sqrt, bias=eps[:, 0:1], scale=scale)

            junk = main[:].rearrange("p b c -> p (b c)")
            for h in range(2):
                sc.wait_ge(x_loaded[h], 16)
                if h:
                    sc.wait_ge(row_sq, 1)
                nc.scalar.activation(junk, stage[:, h, :], ACT.Square, accum_out=rows[:, h:h + 1]).then_inc(row_sq, 1)
            sc.wait_ge(ident_made, 1)
            sc.wait_ge(row_sq, 2)
            root(rows[:], rows[:], 1.0 / D).then_inc(row_rms, 1)
            sc.wait_ge(vec_T, 1)
            copy(vecs[:], aux[:, 0, 0:V_ALL]).then_inc(vecs_ready, 1)
            sc.wait_ge(lb_diff, 1)
            sigmoid(lbs[:, 0, :], lbs[:, 1, :]).then_inc(lb_ready, 1)
            split(Count(0))
            for n in range(8):
                sc.wait_ge(h_made, n + 1)
                copy(act[:, 2 * n:2 * n + 2, 0, :], h_tmp[n % 2]).then_inc(h_hi, 1)
                if n == 3:
                    split(Count(1))
            split(Count(2))
            split(Count(3))

            def sb_last(p, j):
                if j == 0:
                    sc.wait_ge(w_T, p + 1)
                    copy(att_sb, aux[:, 1:3, 0:3 * P]).then_inc(wt_ready, 1)
                    sc.wait_ge(v_T, p + 1)
                    copy(vnat, aux[:, 0, :].rearrange("p (h s v) -> p h s v", h=2, s=2)).then_inc(vnat_ready, 1)
                if j == 1:
                    sc.wait_ge(sb_pv, p + 1)
                    copy(mid[:, 8 + 2 * p:10 + 2 * p, 0, :], aux[:, 3, :].rearrange("p (h t) -> p h t", h=2)
                         ).then_inc(sb_hi, 1)

            for p in range(PAIRS):
                for j in range(SB_SLOTS):
                    s, job = Count(SB_SLOTS * p + j), Count(SB_JOBS * p + j // 2)
                    if j % 2:
                        take_cross(s, job)
                    split(s + RING)
                    if j == 4:
                        if p == 0:
                            sc.wait_ge(pads_made, 1)
                        sc.wait_ge(z_done, p + 1)
                        scale = float(P) ** -0.5
                        sigmoid(sg2[:, :, 0:P], aux[:, 1:3, 0:P], scale)
                        sigmoid(sg2[:, :, P + 1:W2 - 1], aux[:, 1:3, P:3 * P], scale)
                        sigmoid(kp2[:, :, 0:P], aux[:, 1:3, 0:P], -scale)
                        sigmoid(kp2[:, :, P + 1:W2 - 1], aux[:, 1:3, P:3 * P], -scale).then_inc(sb_sig, 1)
                    if p > 0:
                        sb_last(p - 1, j)

            def hg_own(p, j):
                s, job = p.times(HG_SLOTS) + (S_HG + j), p.times(HG_JOBS) + (J_HG + j // 2)
                if j % 2:
                    take_cross(s, job)
                split(s + RING)
                if j == 1:
                    need(sc, job_emptied, job + 1)
                    sigmoid(k, k).then_inc(f_sig, 1)
                if j == 3:
                    need(sc, job_emptied, job + 1)
                    sigmoid(q, xl[1]).then_inc(q_sig, 1)
                if j == 6:
                    need(sc, v_T, p + (PAIRS + 1))
                    copy(vnat, aux[:, 0, :].rearrange("p (h s v) -> p h s v", h=2, s=2)).then_inc(vnat_ready, 1)
                if j == 7:
                    need(sc, job_emptied, job + 1)
                    sigmoid(vT, gate).then_inc(g_sig, 1)

            def hg_last(p, j):
                if j == 0:
                    need(sc, level_done, p.times(LEVELS + 1) + (LEVELS + 1))
                    copy(att_cross, aux[:, 2, 0:2 * P].rearrange("p (h t) -> p h t", h=2)).then_inc(cross_att, 1)
                if j == 1:
                    need(sc, hg_pv, p + 1)
                    nc.scalar.activation(xl[0], aux[:, 0, :].rearrange("p (h t) -> p h t", h=2),
                                         ACT.Square).then_inc(hg_sq, 1)
                if j == 2:
                    need(sc, hg_mean, p + 1)
                    root(suf, aux[:, 3, :].rearrange("p (h t) -> p h t", h=2), 1.0 / P).then_inc(hg_rms, 1)
                if j == 3:
                    need(sc, hg_o, p + 1)
                    copy(mid[:, tiles_of(p), 0, :], xl[0]).then_inc(hg_hi, 1)

            for j in range(HG_SLOTS):
                hg_own(Count(0), j)
                sb_last(PAIRS - 1, j)
            with sc.Fori(1, PAIRS) as i:
                for j in range(HG_SLOTS):
                    hg_own(Count(0, 1, i), j)
                    hg_last(Count(-1, 1, i), j)

            def square(pair_no):
                nc.scalar.activation(sq, xT[:, both(pair_no), :], ACT.Square).then_inc(sq_ready, 1)

            def out_rows(m):
                sc.wait_ge(o_T, m + 1)
                copy(stage[:, :, m * COLS:(m + 1) * COLS],
                     aux[:, 1 + m % 2, :].rearrange("p (h d) -> p h d", h=2)).then_inc(o_copied, 1)

            def prepare(layer, pair_no):
                for c in range(2):
                    tile = pair_no + c
                    ins = nc.scalar.mul(act[:, one(tile), 0, :], xT[:, one(tile), :],
                                        vecs[:, one(tile + V_FFN + DT * layer)])
                ins.then_inc(next_hi, 1)

            for j in range(8):
                split(Count(S_OUTB + j + RING))
                hg_last(Count(PAIRS - 1), j)
            with sc.Fori(0, 2) as i:
                for j in range(4):
                    need(sc, job_emptied, Count(J_OUTA + j + 1, 4, i))
                    need(sc, sumsq, Count(j + 1, 4, i))
                    split(Count(S_OUTA + j + RING, 4, i))
                    prepare(0, Count(2 * j, 8, i))
                    square(Count(2 * j, 8, i))

            def unit(s, job, u):
                split(s + RING)
                take_cross(s + 1, job)
                split(s + (RING + 1))
                need(sc, t_scaled, u + 1)
                sigmoid(sig, tgate).then_inc(t_sig, 1)
                split(s + (RING + 2))
                take_cross(s + 3, job + 1)
                split(s + (RING + 3))
                need(sc, u_made, u + 1)

            def hidden_hi(u_local):
                copy(mid[:, both(u_local), 0, :], tup).then_inc(g_hi, 1)

            def mean_root(n):
                sc.wait_ge(mean_done, n + 1)
                root(rstd[:], aux[:, 0, 0:TOKENS], 1.0 / D).then_inc(rms_done, 1)

            for layer, (s_ffn, j_ffn) in enumerate(((S_FFN0, J_FFN0), (S_FFN1, J_FFN1))):
                if layer == 1:
                    mean_root(1)

                    def pool_hi_of(g):
                        sc.wait_ge(pooled, g + 1)
                        copy(act[:, 4 * g:4 * g + 4, 0, :], pb[POOL_OUT[g]][:, :, 16:]).then_inc(pool_hi, 1)

                    pool_hi_of(0)
                    pool_hi_of(1)
                    for j in range(8):
                        split(Count(S_POOL + j + RING))
                        if j in (1, 3):
                            pool_hi_of(2 + j // 2)
                        if j > 0:
                            sc.wait_ge(slot_used, S_POOL + j + 1)
                            prepare(1, Count(2 * (j - 1)))
                        sc.wait_ge(job_emptied, J_POOL + j + 1)
                        sc.wait_ge(sumsq, 9 * 2 + j + 1)
                        square(Count(2 * j))
                    prepare(1, Count(14))
                for g, (s0, j0, u0, n) in enumerate(ffn_groups(s_ffn, j_ffn)):
                    first = 0
                    ub = sum(UNITS) * layer + u0
                    if g == 0:
                        mean_root(2 * layer)
                        unit(Count(s0), Count(j0), Count(ub))
                        hidden_hi(Count(0))
                        first = 1
                    with sc.Fori(first, n) as i:
                        unit(Count(s0, 4, i), Count(j0, 2, i), Count(ub, 1, i))
                        hidden_hi(Count(0, 2, i))
                    s1, j1 = s0 + 4 * n, j0 + 2 * n
                    last = g == len(UNITS) - 1
                    if not (last and layer == 1):
                        with sc.Fori(0, 4) as i:
                            for j in range(4):
                                if last and j % 2:
                                    need(sc, job_emptied, Count(j1 + j // 2 + 1, 2, i))
                                    need(sc, sumsq, Count(9 + j // 2 + 1, 2, i))
                                split(Count(s1 + j + RING, 4, i))
                                if last and j % 2:
                                    square(Count(2 * (j // 2), 4, i))
                        continue
                    for m in range(8):
                        for j in range(2):
                            if s1 + 2 * m + j + RING < SLOTS:
                                split(Count(s1 + 2 * m + j + RING))
                        sc.wait_ge(job_emptied, j1 + m + 1)
                        sc.wait_ge(sumsq, 9 * 3 + m + 1)
                        square(Count(2 * m))
                        if m > 0:
                            out_rows(m - 1)
                    out_rows(7)
            sc.wait_ge(mean_done, 4)
            root(rows[:], aux[:, 3, 0:2], 1.0 / D).then_inc(row_rms, 1)
            sc.wait_ge(row_rstd, 2)
            for c in range(2):
                nc.scalar.mul(stage[:, 1, c * 1024:(c + 1) * 1024], stage[:, 1, c * 1024:(c + 1) * 1024],
                              rows[:, 1:2]).then_inc(out_scaled[1], 1)

        @block.vector
        def _(ve):
            V = nc.vector
            chain = Chain(ve, dve_chain)

            def mul(out_, a, b):
                return V.tensor_tensor(out_, a, b, ALU.mult)

            def split(s):
                need(ve, hi_ready, s + 1)
                V.tensor_tensor(lo[:, s.place, :], raw[:, s.place, :], hi[:, s.place, :].bitcast(F32),
                                ALU.subtract).then_inc(lo_ready, 1)

            def empty(out_, s, job, crosses):
                need(ve, cross_ready, crosses + 1)
                V.tensor_tensor(out_, bank(job)[:, :, 0:TOKENS], cross[:], ALU.add).then_inc(job_emptied, 1)

            def add_residual(s, job, pair_no, scale=None):
                need(ve, slot_used, s + 1)
                xs = xT[:, both(pair_no), :]
                for half in range(2):
                    ps = bank(job)[:, :, half * TOKENS:(half + 1) * TOKENS]
                    if scale is None:
                        ins = V.tensor_tensor(xs, xs, ps, ALU.add)
                    else:
                        for c in range(2):
                            xc = xT[:, pair_no.base + c, :]
                            at = scale + pair_no.base + c
                            ins = V.scalar_tensor_tensor(xc, ps[:, c, :], vecs[:, at:at + 1], xc, ALU.mult, ALU.add)
                            if (half, c) == (0, 0):
                                chain.link(ins)
                    if half == 0:
                        chain.link(ins)
                        chain.settle()
                ins.then_inc(job_emptied, 1)

            def prepare(layer, prepared, pair_no):
                need(ve, next_hi, prepared + 1)
                for c in range(2):
                    tile = pair_no + c
                    ins = V.scalar_tensor_tensor(act[:, one(tile), 1, :], xT[:, one(tile), :],
                                                 vecs[:, one(tile + V_FFN + DT * layer)],
                                                 act[:, one(tile), 0, :].bitcast(F32), ALU.mult, ALU.subtract)
                    if c == 0:
                        chain.link(ins)
                ins.then_inc(next_ready, 1)

            for n in range(8):
                ve.wait_ge(x_T, n + 1)
                V.tensor_copy(xT[:, 2 * n:2 * n + 2, :],
                              aux[:, 1 + n % 2, :].rearrange("p (c t) -> p c t", c=2)).then_inc(x_copied, 1)
            ve.wait_ge(row_rms, 1)
            V.reciprocal(rows[:], rows[:]).then_inc(row_rstd, 1)
            ve.wait_ge(row_rstd, 1)
            for h in range(2):
                V.tensor_scalar(diag[:, h, :], ident[:], rows[:, h:h + 1], None, ALU.mult).then_inc(diag_ready, 1)
            ve.wait_ge(vecs_ready, 1)
            V.tensor_tensor(lbs[:, 1, :], vecs[:, V_LB:V_LB + HEADS], vecs[:, V_LB + HEADS:V_LB + 2 * HEADS],
                            ALU.subtract).then_inc(lb_diff, 1)
            ve.wait_ge(rstd_bc, 1)
            chain.link(V.tensor_copy(rstd[:], aux[:, 3, 0:TOKENS]))
            chain.settle()

            def make_h(n):
                if n >= 2:
                    ve.wait_ge(h_hi, n - 1)
                    ve.wait_ge(h_ready, n - 1)
                for c in range(2):
                    ins = V.scalar_tensor_tensor(h_tmp[n % 2][:, c, :], xT[:, 2 * n + c, :],
                                                 vecs[:, V_MIX + 2 * n + c:V_MIX + 2 * n + c + 1], rstd[:],
                                                 ALU.mult, ALU.mult)
                    if c == 0:
                        chain.link(ins)
                ins.then_inc(h_made, 1)

            make_h(0)
            for n in range(8):
                if n < 7:
                    make_h(n + 1)
                ve.wait_ge(h_hi, n + 1)
                V.tensor_tensor(act[:, 2 * n:2 * n + 2, 1, :], h_tmp[n % 2],
                                act[:, 2 * n:2 * n + 2, 0, :].bitcast(F32), ALU.subtract).then_inc(h_ready, 1)
                if n == 3:
                    split(Count(0))
            split(Count(1))
            split(Count(2))
            split(Count(3))
            ve.wait_ge(lb_ready, 1)
            chain.link(V.tensor_scalar(lbs[:, 1, :], lbs[:, 0, :], -1.0, 1.0, ALU.mult, ALU.add))

            def sb_last(p, j):
                if j == 1:
                    ve.wait_ge(sb_hi, p + 1)
                    V.tensor_tensor(mid[:, 8 + 2 * p:10 + 2 * p, 1, :],
                                    aux[:, 3, :].rearrange("p (h t) -> p h t", h=2),
                                    mid[:, 8 + 2 * p:10 + 2 * p, 0, :].bitcast(F32), ALU.subtract).then_inc(sb_out, 1)

            for p in range(PAIRS):
                for j in range(SB_SLOTS):
                    s, job = Count(SB_SLOTS * p + j), Count(SB_JOBS * p + j // 2)
                    if j == 1:
                        need(ve, z_done, p)
                        empty(q, s, job, job)
                    if j == 3:
                        empty(k, s, job, job)
                    if j == 5:
                        need(ve, v_T, p)
                        empty(vT, s, job, job)
                    split(s + RING)
                    if j == 4:
                        ve.wait_ge(sb_sig, p + 1)
                        for at in (0, P + 1 + P):
                            a, b = kp2[:, :, at:at + P], sg2[:, :, at:at + P]
                            chain.link(V.tensor_tensor(a, a, tri[:, 1:2, :].to_broadcast((P, 2, P)), ALU.max))
                            chain.link(V.tensor_tensor(b, b, tri[:, 0:1, :].to_broadcast((P, 2, P)), ALU.mult))
                        chain.settle()
                        chain.link(V.tensor_tensor_scan(cum[:, ::-1], kp[:, ::-1], reset[:, ::-1], 0.0,
                                                        ALU.mult, ALU.add))
                        chain.settle()
                        mul(sg[:, 0:2 * W2 - 1], sg[:, 0:2 * W2 - 1], cum[:, 1:2 * W2]).then_inc(w_ready, 1)
                    if p > 0:
                        sb_last(p - 1, j)

            def halves(a, lv):
                return a.rearrange("p h (n two j) -> p (h n) two j", two=2, j=1 << lv)

            def level(p, lv):
                h, n = 1 << lv, TOKENS >> lv
                X, Q, K, A, B = (halves(a, lv) for a in (xl[lv % 2], q, k, pre, suf))
                need(ve, level_done, p.times(LEVELS + 1) + (lv - 1))
                chain.link(mul(X[:, :, 0, :], K[:, :, 0, :], B[:, :, 0, :]))
                if lv > 0:
                    chain.settle()
                mul(X[:, :, 1, :], Q[:, :, 1, :], A[:, :, 1, :]).then_inc(x_level, 1)
                if lv > 1:
                    keep_level(lv - 2)
                if lv < LEVELS:
                    chain.settle()
                    chain.link(mul(B[:, :, 0, :], B[:, :, 0, :], A[:, :, 1, h - 1:h].to_broadcast((P, n, h))))
                    chain.settle()
                    chain.link(mul(A[:, :, 1, :], A[:, :, 1, :], A[:, :, 0, h - 1:h].to_broadcast((P, n, h))))

            def keep_level(lv):
                h = 1 << lv
                o = att_own.rearrange("p g (n two j) -> p g n two j", two=2, j=h)[:, :, :, 1, :]
                m = lmask[:, lv:lv + 1, :].rearrange("p a (n j) -> p a n j", j=h).to_broadcast((P, 4, 64 // h, h))
                d = aux[:, 1 + lv % 2, 0:4 * 64].rearrange("p (g n j) -> p g n j", g=4, j=h)
                V.copy_predicated(o, m.bitcast(U32), d).then_inc(level_kept, 1)

            def hg_own(p, j):
                s, job = p.times(HG_SLOTS) + (S_HG + j), p.times(HG_JOBS) + (J_HG + j // 2)
                if j == 1:
                    need(ve, diag_done, p)
                    if p.stride == 0:
                        ve.wait_ge(w_T, PAIRS)
                    empty(k, s, job, job)
                    split(s + RING)
                    need(ve, f_sig, p + 1)
                    for c in range(2):
                        head = one(p.times(2) + c)
                        chain.link(V.tensor_scalar(pre[:, c, :], k[:, c, :], lbs[:, 1, head], lbs[:, 0, head],
                                                   ALU.mult, ALU.add))
                    chain.settle()
                    V.tensor_scalar(k, pre, -1.0, 1.0, ALU.mult, ALU.add).then_inc(f_ready, 1)
                elif j == 3:
                    empty(xl[1], s, job, job)
                    split(s + RING)
                    chain.link(V.memset(suf, 1.0))
                    need(ve, q_sig, p + 1)
                    mul(q, q, xl[1]).then_inc(q_ready, 1)
                    need(ve, q_ready, p + 1)
                elif j == 5:
                    need(ve, v_T, p + PAIRS)
                    empty(vT, s, job, job)
                    split(s + RING)
                    need(ve, diag_done, p + 1)
                    chain.link(mul(att_own, aux[:, 3, :].rearrange("p (g t) -> p g t", g=4),
                                   ident[:].unsqueeze(1).to_broadcast((P, 4, P))))
                    chain.settle()
                elif j == 7:
                    empty(gate, s, job, job)
                    split(s + RING)
                    need(ve, g_sig, p + 1)
                    mul(gate, gate, vT).then_inc(g_ready, 1)
                else:
                    split(s + RING)
                if j == 4:
                    need(ve, f_ready, p + 1)
                    need(ve, hg_out, p)
                    chain.settle()
                    level(p, 0)
                    level(p, 1)
                if j in (5, 6, 7):
                    level(p, 2 * j - 8)
                    level(p, 2 * j - 7)

            def hg_last(p, j):
                if j == 0:
                    keep_level(LEVELS - 1)
                if j == 2:
                    need(ve, hg_rms, p + 1)
                    need(ve, g_ready, p + 1)
                    chain.link(V.reciprocal(suf, suf))
                    chain.settle()
                    chain.link(mul(xl[0], aux[:, 0, :].rearrange("p (h t) -> p h t", h=2), suf))
                    chain.settle()
                    for c in range(2):
                        ins = V.scalar_tensor_tensor(xl[0][:, c, :], xl[0][:, c, :], vecs[:, V_HGN:V_HGN + 1],
                                                     gate[:, c, :], ALU.mult, ALU.mult)
                        if c == 0:
                            chain.link(ins)
                    ins.then_inc(hg_o, 1)
                if j == 3:
                    need(ve, hg_hi, p + 1)
                    V.tensor_tensor(mid[:, tiles_of(p), 1, :], xl[0], mid[:, tiles_of(p), 0, :].bitcast(F32),
                                    ALU.subtract).then_inc(hg_out, 1)

            for j in range(HG_SLOTS):
                hg_own(Count(0), j)
                sb_last(PAIRS - 1, j)
            with chain.loop(1, PAIRS, HG_LINKS) as i:
                for j in range(HG_SLOTS):
                    if j == 0:
                        need(ve, level_done, Count(LEVELS - (LEVELS + 1), LEVELS + 1, i))
                        need(ve, level_kept, Count(-1, LEVELS, i))
                    hg_own(Count(0, 1, i), j)
                    hg_last(Count(-1, 1, i), j)

            for j in range(8):
                if j == 0:
                    ve.wait_ge(level_done, (LEVELS + 1) * PAIRS - 1)
                    ve.wait_ge(level_kept, LEVELS * PAIRS - 1)
                hg_last(Count(PAIRS - 1), j)
                add_residual(Count(S_OUTB + j), Count(J_OUTB + j), Count(2 * j))
                split(Count(S_OUTB + j + RING))
            with chain.loop(0, 2, 8) as i:
                for j in range(4):
                    add_residual(Count(S_OUTA + j, 4, i), Count(J_OUTA + j, 4, i), Count(2 * j, 8, i))
                    split(Count(S_OUTA + j + RING, 4, i))
                    prepare(0, Count(j, 4, i), Count(2 * j, 8, i))

            rstd2 = rstd[:].unsqueeze(1).to_broadcast((P, 2, TOKENS))

            def unit(s, job, u, c, tile):
                split(s + RING)
                empty(tgate, s + 1, job, c)
                need(ve, job_emptied, job + 1)
                mul(tgate, tgate, rstd2).then_inc(t_scaled, 1)
                split(s + (RING + 1))
                need(ve, t_sig, u + 1)
                chain.link(mul(tgate, tgate, sig))
                split(s + (RING + 2))
                need(ve, hidden, u)
                empty(tup, s + 3, job + 1, c + 1)
                need(ve, job_emptied, job + 2)
                chain.link(mul(tup, tup, rstd2))
                chain.settle()
                mul(tup, tup, tgate).then_inc(u_made, 1)
                split(s + (RING + 3))
                need(ve, g_hi, u + 1)
                V.tensor_tensor(mid[:, both(tile), 1, :], tup, mid[:, both(tile), 0, :].bitcast(F32),
                                ALU.subtract).then_inc(hidden, 1)

            def invert(n):
                ve.wait_ge(rms_done, n)
                chain.link(V.reciprocal(rstd[:], rstd[:]))
                chain.settle()

            for layer, (s_ffn, j_ffn) in enumerate(((S_FFN0, J_FFN0), (S_FFN1, J_FFN1))):
                if layer == 1:
                    chain.link(V.memset(work[:, 0:3 * 1088], 0.0))
                    invert(2)

                    def pool_group(g):
                        win = WINDOWS[g]
                        src, dst = 0, 1
                        if g:
                            chain.settle()
                            ve.wait_ge(pool_ready, g)
                        for c in range(4):
                            t = 4 * g + c
                            chain.link(V.scalar_tensor_tensor(pb[0][:, c, 16:], xT[:, t, :],
                                                              vecs[:, V_MIX + DT + t:V_MIX + DT + t + 1], rstd[:],
                                                              ALU.mult, ALU.mult))
                        w = 1
                        while w < win:
                            chain.settle()
                            chain.link(V.tensor_tensor(pb[dst][:, :, 16:], pb[src][:, :, 16:],
                                                       pb[src][:, :, 16 - w:16 + TOKENS - w], ALU.add))
                            src, dst = dst, 3 - dst
                            w *= 2
                        chain.settle()
                        head = pb[src][:, :, 16:16 + win]
                        chain.link(V.scalar_tensor_tensor(head, head, float(win),
                                                          inv[:, 0:win].unsqueeze(1).to_broadcast((P, 4, win)),
                                                          ALU.mult, ALU.mult))
                        chain.settle()
                        V.scalar_tensor_tensor(pb[POOL_OUT[g]][:, :, 16:], pb[src][:, :, 16:], 1.0 / win,
                                               pb[0][:, :, 16:], ALU.mult, ALU.subtract).then_inc(pooled, 1)
                        ve.wait_ge(pool_hi, g + 1)
                        V.tensor_tensor(act[:, 4 * g:4 * g + 4, 1, :], pb[POOL_OUT[g]][:, :, 16:],
                                        act[:, 4 * g:4 * g + 4, 0, :].bitcast(F32), ALU.subtract
                                        ).then_inc(pool_ready, 1)

                    pool_group(0)
                    pool_group(1)
                    for j in range(8):
                        add_residual(Count(S_POOL + j), Count(J_POOL + j), Count(2 * j), V_SCALE)
                        split(Count(S_POOL + j + RING))
                        if j in (1, 3):
                            pool_group(2 + j // 2)
                        if j > 0:
                            prepare(1, Count(8 + j - 1), Count(2 * (j - 1)))
                    prepare(1, Count(15), Count(14))
                for g, (s0, j0, u0, n) in enumerate(ffn_groups(s_ffn, j_ffn)):
                    first = 0
                    ub = sum(UNITS) * layer + u0
                    cb = C_FFN + 2 * ub
                    if g == 0:
                        invert(2 * layer + 1)
                        unit(Count(s0), Count(j0), Count(ub), Count(cb), Count(0))
                        first = 1
                    with chain.loop(first, n, 2) as i:
                        unit(Count(s0, 4, i), Count(j0, 2, i), Count(ub, 1, i), Count(cb, 2, i), Count(0, 2, i))
                    s1, j1 = s0 + 4 * n, j0 + 2 * n
                    if not (layer == 1 and g == len(UNITS) - 1):
                        with chain.loop(0, 4, 2) as i:
                            for j in range(4):
                                if j % 2:
                                    add_residual(Count(s1 + j, 4, i), Count(j1 + j // 2, 2, i),
                                                 Count(2 * (j // 2), 4, i))
                                split(Count(s1 + j + RING, 4, i))
                        continue
                    for m in range(8):
                        if s1 + 2 * m + RING < SLOTS:
                            split(Count(s1 + 2 * m + RING))
                        add_residual(Count(s1 + 2 * m + 1), Count(j1 + m), Count(2 * m))
                        ve.wait_ge(job_emptied, j1 + m + 1)
                        need(ve, o_T, m - 1)
                        for c in range(2):
                            ins = V.tensor_scalar(xg[m % 2][:, c, :], xT[:, 2 * m + c, :],
                                                  vecs[:, V_FINAL + 2 * m + c:V_FINAL + 2 * m + c + 1], None, ALU.mult)
                            if c == 0:
                                chain.link(ins)
                        ins.then_inc(xg_ready, 1)
                        if s1 + 2 * m + 1 + RING < SLOTS:
                            split(Count(s1 + 2 * m + 1 + RING))
            ve.wait_ge(row_rms, 2)
            V.reciprocal(rows[:], rows[:]).then_inc(row_rstd, 1)
            ve.wait_ge(row_rstd, 2)
            ve.wait_ge(o_copied, 8)
            for c in range(2):
                V.tensor_scalar(stage[:, 0, c * 1024:(c + 1) * 1024], stage[:, 0, c * 1024:(c + 1) * 1024],
                                rows[:, 0:1], None, ALU.mult).then_inc(out_scaled[0], 1)

        @block.tensor
        def _(pe):
            mm = nc.tensor.matmul

            def slot(s, job, rhs, k0, depth, first, last):
                if first:
                    need(pe, job_emptied, job + (-1))
                need(pe, lo_ready, s + 1)
                for c in range(2):
                    for n in range(depth):
                        at = n * COLS + c * P
                        mm(bank(job)[:, c, :], hi[:, s.place, at:at + P], rhs[:, k0 + n, :, :],
                           start=(first and n == 0), stop=False)
                        ins = mm(bank(job)[:, c, TOKENS:], lo[:, s.place, at:at + P], rhs[:, k0 + n, 0, :],
                                 start=False, stop=(last and n == depth - 1))
                ins.then_inc(slot_used, 1)

            def turn(out_, in_):
                return nc.tensor.transpose(out_, in_, ident[:])

            pe.wait_ge(ident_made, 1)
            pe.wait_ge(vec_loaded, 6 * 16)
            nc.tensor.transpose(aux[:, 0, 0:V_ALL], vrows[0:V_ALL, :], ident[0:V_ALL, 0:V_ALL]).then_inc(vec_T, 1)
            pe.wait_ge(x_loaded[0], 16)
            pe.wait_ge(x_loaded[1], 16)
            for n in range(8):
                need(pe, x_copied, n - 1)
                for c in range(2):
                    for h in range(2):
                        ins = turn(aux[:, 1 + n % 2, c * TOKENS + h * P:c * TOKENS + (h + 1) * P],
                                   stage[:, h, (2 * n + c) * P:(2 * n + c + 1) * P])
                ins.then_inc(x_T, 1)
            pe.wait_ge(diag_ready, 2)
            mm(aux[:, 3, 0:TOKENS], ones[:], diag.rearrange("p h t -> p (h t)"), start=True, stop=True
               ).then_inc(rstd_bc, 1)

            def weigh(o, h, a00, a01, a11, **kw):
                mm(o[:, 0:P], vnat[:, h, 0, :], a00, start=True, stop=False)
                mm(o[:, P:2 * P], vnat[:, h, 0, :], a01, start=False, stop=False)
                return mm(o[:, P:2 * P], vnat[:, h, 1, :], a11, start=False, stop=True)

            def turn_v():
                for h in range(2):
                    for n in range(2):
                        ins = turn(aux[:, 0, (2 * h + n) * P:(2 * h + n + 1) * P], vT[:, h, n * P:(n + 1) * P])
                ins.then_inc(v_T, 1)

            def sb_last(p, j):
                if j == 0:
                    pe.wait_ge(w_ready, p + 1)
                    for h in range(2):
                        for n, at in enumerate((0, P + 1, 2 * P + 1)):
                            ins = turn(aux[:, 1 + h, n * P:(n + 1) * P], sg2[:, h, at:at + P])
                    ins.then_inc(w_T, 1)
                    pe.wait_ge(job_emptied, SB_JOBS * p + 3)
                    turn_v()
                if j == 1:
                    pe.wait_ge(wt_ready, p + 1)
                    pe.wait_ge(vnat_ready, p + 1)
                    need(pe, sb_out, p)
                    for h in range(2):
                        ins = weigh(aux[:, 3, h * TOKENS:(h + 1) * TOKENS], h, *(att[:, h, n, :] for n in range(3)))
                    ins.then_inc(sb_pv, 1)

            for p in range(PAIRS):
                for j in range(SB_SLOTS):
                    if p == 0 and j < 2:
                        pe.wait_ge(h_ready, 4 * (j + 1))
                    slot(Count(SB_SLOTS * p + j), Count(SB_JOBS * p + j // 2), act, DEPTH * (j % 2), DEPTH,
                         j % 2 == 0, j % 2 == 1)
                    if j == 4:
                        pe.wait_ge(job_emptied, SB_JOBS * p + 2)
                        for h in range(2):
                            mm(aux[:, 1 + h, 0:P], q[:, h, 0:P], k[:, h, 0:P], start=True, stop=True)
                            ins = mm(aux[:, 1 + h, P:3 * P], q[:, h, P:], k[:, h, :], start=True, stop=True)
                        ins.then_inc(z_done, 1)
                    if p > 0:
                        sb_last(p - 1, j)

            def level(p, lv):
                need(pe, x_level, p.times(LEVELS + 1) + (lv + 1))
                need(pe, level_kept, p.times(LEVELS) + (lv - 1 if lv else 0))
                if lv == 1:
                    need(pe, cross_att, p)
                X = xl[lv % 2]
                for h in range(2):
                    if lv == LEVELS:
                        ins = mm(aux[:, 2, h * P:(h + 1) * P], X[:, h, 0:P], X[:, h, P:], start=True, stop=True)
                        continue
                    for n in range(2):
                        tile = X[:, h, n * P:(n + 1) * P]
                        upper = tile.rearrange("p (n two j) -> p n two j", two=2, j=1 << lv)[:, :, 1, :]
                        ins = mm(aux[:, 1 + lv % 2, (2 * h + n) * 64:(2 * h + n + 1) * 64], tile, upper,
                                 start=True, stop=True)
                ins.then_inc(level_done, 1)

            def hg_own(p, j):
                s, job = p.times(HG_SLOTS) + (S_HG + j), p.times(HG_JOBS) + (J_HG + j // 2)
                slot(s, job, act, DEPTH * (j % 2), DEPTH, j % 2 == 0, j % 2 == 1)
                if j == 5:
                    need(pe, q_ready, p + 1)
                    need(pe, hg_rms, p)
                    for h in range(2):
                        for n in range(2):
                            ins = mm(aux[:, 3, (2 * h + n) * P:(2 * h + n + 1) * P], k[:, h, n * P:(n + 1) * P],
                                     q[:, h, n * P:(n + 1) * P], start=True, stop=True)
                    ins.then_inc(diag_done, 1)
                    level(p, 0)
                    level(p, 1)
                if j == 6:
                    need(pe, job_emptied, p.times(HG_JOBS) + (J_HG + 3))
                    need(pe, hg_o, p)
                    turn_v()
                    level(p, 2)
                    level(p, 3)
                if j == 7:
                    level(p, 4)
                    level(p, 5)

            def hg_last(p, j):
                if j == 0:
                    level(p, 6)
                    level(p, 7)
                if j == 1:
                    need(pe, level_kept, p.times(LEVELS) + LEVELS)
                    need(pe, cross_att, p + 1)
                    need(pe, vnat_ready, p + (PAIRS + 1))
                    for h in range(2):
                        ins = weigh(aux[:, 0, h * TOKENS:(h + 1) * TOKENS], h,
                                    att_own[:, 2 * h, :], att_cross[:, h, :], att_own[:, 2 * h + 1, :])
                    ins.then_inc(hg_pv, 1)
                if j == 2:
                    need(pe, hg_sq, p + 1)
                    mm(aux[:, 3, :], ones[:], xl[0].rearrange("p h t -> p (h t)"), start=True, stop=True
                       ).then_inc(hg_mean, 1)

            for j in range(HG_SLOTS):
                hg_own(Count(0), j)
                sb_last(PAIRS - 1, j)
            with pe.Fori(1, PAIRS) as i:
                for j in range(HG_SLOTS):
                    hg_own(Count(0, 1, i), j)
                    hg_last(Count(-1, 1, i), j)
            pe.wait_ge(sb_out, PAIRS)
            for j in range(8):
                slot(Count(S_OUTB + j), Count(J_OUTB + j), mid, 8, DEPTH, True, True)
                hg_last(Count(PAIRS - 1), j)
            pe.wait_ge(hg_out, PAIRS)
            with pe.Fori(0, 2) as i:
                for j in range(4):
                    slot(Count(S_OUTA + j, 4, i), Count(J_OUTA + j, 4, i), mid, 0, DEPTH, True, True)

            def mean(n):
                pe.wait_ge(sumsq, 9 * (n + 1))
                for c in range(2):
                    ins = mm(aux[:, 0, 0:TOKENS], ones[:], acc[:, c, :], start=(c == 0), stop=(c == 1))
                ins.then_inc(mean_done, 1)

            for layer, (s_ffn, j_ffn) in enumerate(((S_FFN0, J_FFN0), (S_FFN1, J_FFN1))):
                if layer == 1:
                    mean(1)
                    for j in range(8):
                        pe.wait_ge(pool_ready, j // 2 + 1)
                        slot(Count(S_POOL + j), Count(J_POOL + j), act, 4 * (j // 2), 4, True, True)
                for g, (s0, j0, u0, n) in enumerate(ffn_groups(s_ffn, j_ffn)):
                    first = 0
                    if g == 0:
                        for j in range(4):
                            if j < 2:
                                pe.wait_ge(next_ready, 8 * layer + 4 * (j + 1))
                            slot(Count(s0 + j), Count(j0 + j // 2), act, DEPTH * (j % 2), DEPTH, j % 2 == 0, j % 2 == 1)
                            if j == 0:
                                mean(2 * layer)
                        first = 1
                    with pe.Fori(first, n) as i:
                        for j in range(4):
                            slot(Count(s0 + j, 4, i), Count(j0 + j // 2, 2, i), act, DEPTH * (j % 2), DEPTH,
                                 j % 2 == 0, j % 2 == 1)
                    s1, j1 = s0 + 4 * n, j0 + 2 * n
                    done = sum(UNITS) * layer + u0
                    pe.wait_ge(hidden, done + n // 2)
                    if not (layer == 1 and g == len(UNITS) - 1):
                        with pe.Fori(0, 4) as i:
                            for j in range(4):
                                if j == 1:
                                    pe.wait_ge(hidden, done + n)
                                slot(Count(s1 + j, 4, i), Count(j1 + j // 2, 2, i), mid, n * (j % 2), n,
                                     j % 2 == 0, j % 2 == 1)
                        continue

                    def turn_rows(m):
                        pe.wait_ge(xg_ready, m + 1)
                        need(pe, o_copied, m - 1)
                        for h in range(2):
                            for c in range(2):
                                ins = turn(aux[:, 1 + m % 2, h * TOKENS + c * P:h * TOKENS + (c + 1) * P],
                                           xg[m % 2][:, c, h * P:(h + 1) * P])
                        ins.then_inc(o_T, 1)

                    for m in range(8):
                        for j in range(2):
                            if m == 0 and j == 1:
                                pe.wait_ge(hidden, done + n)
                            slot(Count(s1 + 2 * m + j), Count(j1 + m), mid, n * j, n, j == 0, j == 1)
                            if m > 0 and j == 0:
                                turn_rows(m - 1)
                    turn_rows(7)
                    pe.wait_ge(sumsq, 9 * 4)
                    for h in range(2):
                        for c in range(2):
                            ins = mm(aux[:, 3, h:h + 1], acc[:, c, h * P:(h + 1) * P], ones[:, 0:1],
                                     start=(c == 0), stop=(c == 1))
                    ins.then_inc(mean_done, 1)


_INS = ["x", "mix_norm", "ffn_norm", "final_norm", "ab_w_in", "lb_logits", "hg_out_norm", "ab_w_out",
        "pool_w", "pool_scale", "ffn_w_gate", "ffn_w_up", "ffn_w_down"]


def kernel(**inputs):
    import numpy as np
    from concourse import bacc
    from concourse.bass_utils import run_bass_kernel_spmd

    nc = bacc.Bacc("TRN2", target_bir_lowering=False, num_devices=1)
    arrays, args = {}, []
    for name in _INS:
        a = np.ascontiguousarray(inputs[name])
        arrays[f"in_{name}"] = a
        args.append(nc.dram_tensor(f"in_{name}", a.shape, mybir.dt.from_np(a.dtype), kind="ExternalInput").ap())
    args.append(nc.dram_tensor("out_0", (1, TOKENS, D), F32, kind="ExternalOutput").ap())
    trunk(nc, *args)
    return run_bass_kernel_spmd(nc, [arrays], core_ids=[0]).results[0]["out_0"]
```

```python
from contextlib import ExitStack, contextmanager

import concourse.bass as bass
from concourse import mybir

F32 = mybir.dt.float32
F32R = mybir.dt.float32r
U32 = mybir.dt.uint32
ALU = mybir.AluOpType
ACT = mybir.ActivationFunctionType

P = 128
TOKENS = 256
D = 2048
DT = D // P
FFN = 5632
HEADS = 8
PAIRS = HEADS // 2
EPS = 1e-6
RING = 4
COLS = 256
DEPTH = 8
SLOT = DEPTH * COLS
QA, FA, IA, GA, QB, KB, VB = (1024 * n for n in range(7))
UNITS = (8, 8, 6)
assert sum(UNITS) * COLS == FFN
WINDOWS = (2, 4, 8, 16)
GROUPS = len(WINDOWS)
SPILL = 16
HG_LINKS = 29
LEVELS = 7

SB_SLOTS, SB_JOBS = 6, 3
HG_SLOTS, HG_JOBS = 8, 4
S_HG, J_HG = SB_SLOTS * PAIRS, SB_JOBS * PAIRS
S_OUTB, J_OUTB = S_HG + HG_SLOTS * PAIRS, J_HG + HG_JOBS * PAIRS
S_OUTA, J_OUTA = S_OUTB + 8, J_OUTB + 8
FFN_SLOTS = 4 * sum(UNITS) + 16 * len(UNITS)
FFN_JOBS = 2 * sum(UNITS) + 8 * len(UNITS)
S_FFN0, J_FFN0 = S_OUTA + 8, J_OUTA + 8
S_POOL, J_POOL = S_FFN0 + FFN_SLOTS, J_FFN0 + FFN_JOBS
S_FFN1, J_FFN1 = S_POOL + GROUPS, J_POOL + GROUPS
SLOTS = S_FFN1 + FFN_SLOTS
C_FFN = J_OUTB
PREP_FFN0, PREP_POOL, PREP_FFN1 = 0, 8, 16

V_MIX, V_FFN, V_FINAL, V_SCALE, V_LB, V_HGN, V_ALL = 0, 32, 64, 80, 96, 112, 113


def ffn_groups(s0, j0):
    out, u = [], 0
    for n in UNITS:
        out.append((s0, j0, u, n))
        s0, j0, u = s0 + 4 * n + 16, j0 + 2 * n + 8, u + n
    return out


def down_slots(n_jobs):
    order = [(0, 0), (1, 0), (0, 1), (1, 1)]
    return order + [(m, half) for m in range(2, n_jobs) for half in range(2)]


class Count:

    def __init__(self, base, stride=0, i=0):
        self.base, self.stride, self.i = base, stride, i

    def __add__(self, k):
        return Count(self.base + k, self.stride, self.i)

    def times(self, k):
        return Count(self.base * k, self.stride * k, self.i)

    def lap(self):
        return Count(self.base // RING, self.stride // RING, self.i)

    @property
    def place(self):
        assert self.stride % RING == 0
        return self.base % RING

    @property
    def parity(self):
        assert self.stride % 2 == 0
        return self.base % 2

    @property
    def value(self):
        return self.base + self.i * self.stride if self.stride else self.base


def need(eng, semaphore, count):
    v = count.value if isinstance(count, Count) else count
    if not (isinstance(v, int) and v <= 0):
        eng.wait_ge(semaphore, v)


class Chain:

    def __init__(self, eng, sem):
        self.eng, self.sem, self.base, self.n, self.used = eng, sem, 0, 0, 0

    def link(self, ins):
        ins.then_inc(self.sem, 1)
        self.n += 1

    def settle(self):
        self.eng.wait_ge(self.sem, self.base + self.n)

    @contextmanager
    def loop(self, first, end, per):
        start = self.base + self.n
        with self.eng.Fori(first, end) as i:
            self.base, self.n = i * per + (start - first * per), 0
            yield i
            assert self.n == per, f"{self.n} links in a loop's body"
        self.base, self.n = start + (end - first) * per, 0


def one(tile):
    v = tile.value if isinstance(tile, Count) else tile
    return slice(v, v + 1) if isinstance(v, int) else bass.ds(v, 1)


def both(tile):
    v = tile.value
    return slice(v, v + 2) if isinstance(v, int) else bass.ds(v, 2)


def tiles_of(p):
    return both(p.times(2))


def trunk(nc, x, mix_norm, ffn_norm, final_norm, ab_w_in, lb_logits, hg_out_norm, ab_w_out,
          pool_w, pool_scale, w_gate, w_up, w_down, out):
    with ExitStack() as ctx:
        def sb(name, shape, dt=F32):
            return ctx.enter_context(nc.sbuf_tensor(name, shape, dt))

        def sem(name):
            return ctx.enter_context(nc.semaphore(name))

        def semaphores(name, n):
            return [sem(f"{name}{i}") for i in range(n)]

        raw = sb("raw", [P, RING, SLOT])
        hi = sb("hi", [P, RING, SLOT], F32R)
        lo = sb("lo", [P, RING, SLOT], F32R)
        xT = sb("xT", [P, DT, TOKENS])
        act = sb("act", [P, DT, 2, TOKENS], F32R)
        mid = sb("mid", [P, DT, 2, TOKENS], F32R)
        ident = sb("ident", [P, P])
        ones = sb("ones", [P, P])
        vecs = sb("vecs", [P, V_ALL])
        vrows = sb("vrows", [P, P])
        lbs = sb("lbs", [P, 2, HEADS])
        eps = sb("eps", [P, 1])
        rows = sb("rows", [P, 2])
        z_scale = sb("z_scale", [P, 2, 2])
        rstd = sb("rstd", [P, TOKENS])
        rstd2 = rstd[:].unsqueeze(1).to_broadcast((P, 2, TOKENS))
        cross = sb("cross", [P, 2, TOKENS])
        tri = sb("tri", [P, 2, P])
        lmask = sb("lmask", [P, LEVELS, 64])
        work = sb("work", [P, 5904])

        def pair(a):
            return work[:, a:a + 512].rearrange("p (c t) -> p c t", c=2)

        q, k, vT = pair(0), pair(512), pair(1024)
        xg = [pair(5120), cross[:]]
        vnat = work[:, 1536:2048].rearrange("p (h s v) -> p h s v", h=2, s=2)
        att = work[:, 2048:2816].rearrange("p (h b t) -> p h b t", h=2, b=3)
        att_sb = work[:, 2048:2816].rearrange("p (h t) -> p h t", h=2)
        att_own = work[:, 2048:2560].rearrange("p (g t) -> p g t", g=4)
        att_cross = work[:, 2560:2816].rearrange("p (h t) -> p h t", h=2)
        W2 = 386
        sg = work[:, 2816:2816 + 772]
        kp = work[:, 3588:3588 + 772]
        cum = work[:, 4360:4360 + 772]
        reset = work[:, 5132:5132 + 772]
        sg2, kp2, reset2 = (a.rearrange("p (h w) -> p h w", h=2) for a in (sg, kp, reset))
        pre, suf, gate = pair(2816), pair(3328), pair(4864)
        xl = [pair(3840), pair(4352)]
        tgate, sig, tup = pair(0), pair(512), pair(1024)
        acc, sq = pair(4096), pair(4608)
        zt = [work[:, a:a + 1024].rearrange("p (h d) -> p h d", h=2) for a in (2624, 0)]
        window = work[:, 1536:1536 + GROUPS * (TOKENS + SPILL)].rearrange("p (g t) -> p g t", g=GROUPS)
        stage = work[:, 0:4096].rearrange("p (h d) -> p h d", h=2)
        diag = work[:, 1536:1792].rearrange("p (h t) -> p h t", h=2)
        junk = mid[:, 0:4, :, :].rearrange("p a b t -> p (a b t)")

        main = ctx.enter_context(nc.psum_tensor("main", [P, 4, 512], F32))
        aux = ctx.enter_context(nc.psum_tensor("aux", [P, 4, 512], F32))

        def start_bank(n):
            return (main if n < 4 else aux)[:, n % 4, :].rearrange("p (c t) -> p c t", c=2)

        def bank(job):
            return main[:, 2 * job.parity:2 * job.parity + 2, :]

        x_loaded, raw_loaded = semaphores("x_loaded", 2), semaphores("raw_loaded", RING)
        out_scaled = semaphores("out_scaled", 2)
        ident_made = sem("ident_made")
        pads_made = sem("pads_made")
        sumsq = sem("sumsq")
        hi_ready = sem("hi_ready")
        cross_ready = sem("cross_ready")
        row_sq = sem("row_sq")
        row_rms = sem("row_rms")
        vec_T = sem("vec_T")
        vecs_ready = sem("vecs_ready")
        lb_diff = sem("lb_diff")
        lb_ready = sem("lb_ready")
        h_hi = sem("h_hi")
        wt_ready = sem("wt_ready")
        vnat_ready = sem("vnat_ready")
        sb_hi = sem("sb_hi")
        sb_sig = sem("sb_sig")
        f_sig = sem("f_sig")
        q_sig = sem("q_sig")
        g_sig = sem("g_sig")
        cross_att = sem("cross_att")
        hg_sq = sem("hg_sq")
        hg_rms = sem("hg_rms")
        hg_hi = sem("hg_hi")
        g_hi = sem("g_hi")
        sq_ready = sem("sq_ready")
        q_ready = sem("q_ready")
        next_hi = sem("next_hi")
        t_sig = sem("t_sig")
        rms_done = sem("rms_done")
        z_kept = sem("z_kept")
        lo_ready = sem("lo_ready")
        job_emptied = sem("job_emptied")
        next_ready = sem("next_ready")
        x_copied = sem("x_copied")
        row_rstd = sem("row_rstd")
        diag_ready = sem("diag_ready")
        g_ready = sem("g_ready")
        rstd_bc = sem("rstd_bc")
        z_scale_made = sem("z_scale_made")
        divided = sem("divided")
        h_ready = sem("h_ready")
        sb_out = sem("sb_out")
        w_ready = sem("w_ready")
        x_level = sem("x_level")
        level_kept = sem("level_kept")
        f_ready = sem("f_ready")
        hg_o = sem("hg_o")
        hg_out = sem("hg_out")
        t_scaled = sem("t_scaled")
        u_made = sem("u_made")
        hidden = sem("hidden")
        x_mixed = sem("x_mixed")
        windows_made = sem("windows_made")
        mix_done = sem("mix_done")
        xg_ready = sem("xg_ready")
        slot_used = sem("slot_used")
        x_T = sem("x_T")
        v_T = sem("v_T")
        w_T = sem("w_T")
        sb_pv = sem("sb_pv")
        z_done = sem("z_done")
        level_done = sem("level_done")
        diag_done = sem("diag_done")
        hg_pv = sem("hg_pv")
        hg_mean = sem("hg_mean")
        mean_done = sem("mean_done")
        o_T = sem("o_T")
        out_stored = sem("out_stored")
        dve_chain = sem("dve_chain")
        o_copied = sem("o_copied")
        vec_loaded = sem("vec_loaded")
        pool_chain = sem("pool_chain")
        block = ctx.enter_context(nc.Block())

        @block.sync
        def _(sp):
            rows_of = [(mix_norm.rearrange("l (t p) -> (l t) p", p=P), V_MIX, 32),
                       (ffn_norm.rearrange("l (t p) -> (l t) p", p=P), V_FFN, 32),
                       (final_norm.rearrange("(t p) -> t p", p=P), V_FINAL, 16),
                       (pool_scale.rearrange("l (t p) -> (l t) p", p=P), V_SCALE, 16),
                       (lb_logits.rearrange("l (t p) -> (l t) p", p=P), V_LB, 16),
                       (hg_out_norm, V_HGN, 1)]
            for h in range(2):
                sp.dma_start(stage[:, h, :], x[0, h * P:(h + 1) * P, :]).then_inc(x_loaded[h], 16)
            for src, at, n in rows_of:
                sp.dma_start(vrows[at:at + n, :], src).then_inc(vec_loaded, 16)

            def load(s, src, depth):
                need(sp, lo_ready, s + (1 - RING))
                size = depth * src.shape[-1]
                dst = raw[:, s.place, 0:size].rearrange("p (k c) -> p k c", k=depth)
                sp.dma_start(dst, src).then_inc(raw_loaded[s.place], 16)

            def block_rows(w, row, depth, col):
                return w[row:row + depth * P, bass.ds(col, COLS)].rearrange("(k p) c -> p k c", p=P)

            for p in range(PAIRS):
                for n, part in enumerate((QB, KB, VB)):
                    for half in range(2):
                        load(Count(SB_SLOTS * p + 2 * n + half),
                             block_rows(ab_w_in[0], 1024 * half, DEPTH, part + COLS * p), DEPTH)
            with sp.Fori(1, PAIRS + 1) as p:
                for n, part in enumerate((FA, QA, IA, GA)):
                    for half in range(2):
                        load(Count(S_HG + 2 * n + half - HG_SLOTS, HG_SLOTS, p),
                             block_rows(ab_w_in[0], 1024 * half, DEPTH, p * COLS + (part - COLS)), DEPTH)
            for s0, row in ((S_OUTB, 1024), (S_OUTA, 0)):
                with sp.Fori(1, 3) as i:
                    for j in range(4):
                        load(Count(s0 + j - 4, 4, i),
                             block_rows(ab_w_out[0], row, DEPTH, i * (4 * COLS) + (j - 4) * COLS), DEPTH)
            for layer, s_ffn in enumerate((S_FFN0, S_FFN1)):
                if layer == 1:
                    for g in range(GROUPS):
                        load(Count(S_POOL + g), pool_w[0, g].rearrange("(k p) c -> p k c", p=P), 4)
                for s0, j0, u0, n in ffn_groups(s_ffn, 0):
                    if u0 == 0:
                        for j, (half, w) in enumerate(((0, w_gate), (0, w_up), (1, w_gate), (1, w_up))):
                            load(Count(s0 + j), block_rows(w[layer], 1024 * half, DEPTH, 0), DEPTH)
                    with sp.Fori(2 if u0 == 0 else 1, n + 1) as i:
                        for m, w in enumerate((w_gate, w_up)):
                            for half in range(2):
                                load(Count(s0 + 2 * m + half - 4, 4, i),
                                     block_rows(w[layer], 1024 * half, DEPTH, i * COLS + (u0 - 1) * COLS), DEPTH)
                    if u0 + n == sum(UNITS):
                        for j, (m, half) in enumerate(down_slots(8)):
                            load(Count(s0 + 4 * n + j),
                                 block_rows(w_down[layer], (2 * u0 + n * half) * P, n, m * COLS), n)
                        continue
                    with sp.Fori(1, 5) as i:
                        for j, (m, half) in enumerate(down_slots(2)):
                            load(Count(s0 + 4 * n + j - 4, 4, i),
                                 block_rows(w_down[layer], (2 * u0 + n * half) * P, n,
                                            i * (2 * COLS) + (m - 2) * COLS), n)
            for c in range(2):
                for h in range(2):
                    sp.wait_ge(out_scaled[h], c + 1)
                    sp.dma_start(out[0, h * P:(h + 1) * P, c * 1024:(c + 1) * 1024],
                                 stage[:, h, c * 1024:(c + 1) * 1024]).then_inc(out_stored, 16)
            sp.wait_ge(out_stored, 4 * 16)

        @block.gpsimd
        def _(pool):
            chain = Chain(pool, pool_chain)
            chain.link(nc.gpsimd.memset(ident[:], 0.0))
            chain.link(nc.gpsimd.memset(ones[:], 1.0))
            chain.link(nc.gpsimd.memset(tri[:], 1.0))
            chain.link(nc.gpsimd.memset(lmask[:], 1.0))
            chain.link(nc.gpsimd.memset(eps[:], EPS))
            chain.settle()
            nc.gpsimd.affine_select(out=ident[:], in_=ident[:], compare_op=ALU.not_equal, fill=1.0, base=0,
                                    pattern=[[-1, P]], channel_multiplier=1).then_inc(ident_made, 1)
            chain.link(nc.gpsimd.affine_select(out=tri[:, 0, :], in_=tri[:, 0, :], compare_op=ALU.is_gt, fill=0.0,
                                               base=0, pattern=[[-1, P]], channel_multiplier=1))
            chain.link(nc.gpsimd.affine_select(out=tri[:, 1, :], in_=tri[:, 1, :], compare_op=ALU.is_ge, fill=0.0,
                                               base=0, pattern=[[1, P]], channel_multiplier=-1))
            for lv in range(LEVELS):
                h = 1 << lv
                m = lmask[:, lv, :].rearrange("p (n j) -> p n j", j=h)
                chain.link(nc.gpsimd.affine_select(out=m, in_=m, compare_op=ALU.is_ge, fill=0.0, base=0,
                                                   pattern=[[-2 * h, 64 // h], [0, h]], channel_multiplier=1))
            chain.settle()
            for lv in range(LEVELS):
                h = 1 << lv
                m = lmask[:, lv, :].rearrange("p (n j) -> p n j", j=h)
                chain.link(nc.gpsimd.affine_select(out=m, in_=m, compare_op=ALU.is_ge, fill=0.0, base=h - 1,
                                                   pattern=[[2 * h, 64 // h], [0, h]], channel_multiplier=-1))

            pool.wait_ge(x_T, 8)
            pool.wait_ge(row_sq, 2)
            chain.link(nc.gpsimd.memset(sg, 0.0))
            chain.link(nc.gpsimd.memset(kp, 0.0))
            chain.link(nc.gpsimd.memset(reset, 0.0))
            chain.settle()
            chain.link(nc.gpsimd.memset(reset2[:, :, P:P + 1], 1.0))
            nc.gpsimd.memset(reset2[:, :, W2 - 1:W2], 1.0).then_inc(pads_made, 1)

            for n in range(4):
                if n == 0:
                    pool.wait_ge(hg_out, PAIRS)
                else:
                    pool.wait_ge(mean_done, n)
                nc.gpsimd.memset(acc, 0.0).then_inc(sumsq, 1)
                with pool.Fori(0, 8) as i:
                    pool.wait_ge(sq_ready, i + (8 * n + 1))
                    pool.wait_ge(sumsq, i + (9 * n + 1))
                    nc.gpsimd.tensor_tensor(acc, acc, sq, ALU.add).then_inc(sumsq, 1)
                if n > 0:
                    continue
                for g, w in enumerate(WINDOWS):
                    chain.link(nc.gpsimd.memset(window[:, g, :], 1.0 / w))
                chain.settle()
                for g, w in enumerate(WINDOWS):
                    for t in range(w - 1):
                        chain.link(nc.gpsimd.memset(window[:, g, t:t + 1], 1.0 / (t + 1)))
                tiles = ((0, P + SPILL), (P + SPILL, P))
                chain.settle()
                for g in range(GROUPS):
                    for at, width in tiles:
                        m = window[:, g, at:at + width]
                        chain.link(nc.gpsimd.affine_select(out=m, in_=m, compare_op=ALU.is_ge, fill=0.0, base=0,
                                                           pattern=[[1, width]], channel_multiplier=-1))
                chain.settle()
                for g, w in enumerate(WINDOWS):
                    for at, width in tiles:
                        m = window[:, g, at:at + width]
                        chain.link(nc.gpsimd.affine_select(out=m, in_=m, compare_op=ALU.is_ge, fill=0.0, base=w - 1,
                                                           pattern=[[-1, width]], channel_multiplier=1))
                chain.settle()
                for g in range(GROUPS):
                    for at, width in tiles:
                        m = window[:, g, at:at + P]
                        nc.gpsimd.tensor_tensor(m, m, ident[:], ALU.subtract).then_inc(windows_made, 1)

        @block.scalar
        def _(sc):
            def copy(out_, in_):
                return nc.scalar.copy(out_, in_)

            def split(s):
                need(sc, raw_loaded[s.place], (s.lap() + 1).times(16))
                need(sc, slot_used, s + (1 - RING))
                copy(hi[:, s.place, :], raw[:, s.place, :]).then_inc(hi_ready, 1)

            def take_cross(s, job):
                need(sc, slot_used, s + 1)
                need(sc, job_emptied, job)
                copy(cross[:], bank(job)[:, :, TOKENS:]).then_inc(cross_ready, 1)

            def sigmoid(out_, in_, scale=1.0):
                return nc.scalar.activation(out_, in_, ACT.Sigmoid, scale=scale)

            def root(out_, in_, scale):
                return nc.scalar.activation(out_, in_, ACT.Sqrt, bias=eps[:, 0:1], scale=scale)

            sc.wait_ge(vec_T, 1)
            copy(vecs[:], aux[:, 3, 0:V_ALL]).then_inc(vecs_ready, 1)
            sc.wait_ge(vecs_ready, 1)
            for n in range(8):
                sc.wait_ge(x_T, n + 1)
                for c in range(2):
                    ins = nc.scalar.mul(act[:, 2 * n + c, 0, :], start_bank(n)[:, c, :],
                                        vecs[:, V_MIX + 2 * n + c:V_MIX + 2 * n + c + 1])
                ins.then_inc(h_hi, 1)
                if n == 3:
                    split(Count(0))
            split(Count(1))
            split(Count(2))
            for h in range(2):
                sc.wait_ge(x_loaded[h], 16)
                if h:
                    sc.wait_ge(row_sq, 1)
                nc.scalar.activation(junk, stage[:, h, :], ACT.Square, accum_out=rows[:, h:h + 1]).then_inc(row_sq, 1)
            split(Count(3))
            sc.wait_ge(ident_made, 1)
            sc.wait_ge(row_sq, 2)
            root(rows[:], rows[:], 1.0 / D).then_inc(row_rms, 1)
            sc.wait_ge(lb_diff, 1)
            sigmoid(lbs[:, 0, :], lbs[:, 1, :]).then_inc(lb_ready, 1)

            def values():
                v_of = aux[:, 0, :].rearrange("p (h s v) -> p h s v", h=2, s=2)
                for n in range(2):
                    ins = nc.scalar.mul(vnat[:, :, n, :], v_of[:, :, n, :], rows[:, n:n + 1])
                ins.then_inc(vnat_ready, 1)

            def sb_last(p, j):
                if j == 0:
                    sc.wait_ge(w_T, p + 1)
                    copy(att_sb, aux[:, 1:3, 0:3 * P]).then_inc(wt_ready, 1)
                    sc.wait_ge(v_T, p + 1)
                    if p == 0:
                        sc.wait_ge(row_rstd, 1)
                    values()
                if j == 1:
                    sc.wait_ge(sb_pv, p + 1)
                    copy(mid[:, 8 + 2 * p:10 + 2 * p, 0, :], aux[:, 3, :].rearrange("p (h t) -> p h t", h=2)
                         ).then_inc(sb_hi, 1)

            for p in range(PAIRS):
                for j in range(SB_SLOTS):
                    s, job = Count(SB_SLOTS * p + j), Count(SB_JOBS * p + j // 2)
                    if j % 2:
                        take_cross(s, job)
                    split(s + RING)
                    if j == 4:
                        if p == 0:
                            sc.wait_ge(pads_made, 1)
                            sc.wait_ge(z_scale_made, 2)
                        sc.wait_ge(z_done, p + 1)
                        sigmoid(sg2[:, :, 0:P], aux[:, 1:3, 0:P], z_scale[:, 0, 0:1])
                        sigmoid(sg2[:, :, P + 1:W2 - 1], aux[:, 1:3, P:3 * P], z_scale[:, 0, 1:2])
                        sigmoid(kp2[:, :, 0:P], aux[:, 1:3, 0:P], z_scale[:, 1, 0:1])
                        sigmoid(kp2[:, :, P + 1:W2 - 1], aux[:, 1:3, P:3 * P], z_scale[:, 1, 1:2]).then_inc(sb_sig, 1)
                    if p > 0:
                        sb_last(p - 1, j)

            def hg_own(p, j):
                s, job = p.times(HG_SLOTS) + (S_HG + j), p.times(HG_JOBS) + (J_HG + j // 2)
                if j % 2:
                    take_cross(s, job)
                split(s + RING)
                if j == 1:
                    need(sc, divided, p.times(3) + (PAIRS + 1))
                    sigmoid(k, k).then_inc(f_sig, 1)
                if j == 3:
                    need(sc, divided, p.times(3) + (PAIRS + 2))
                    sigmoid(q, xl[1]).then_inc(q_sig, 1)
                if j == 6:
                    need(sc, v_T, p + (PAIRS + 1))
                    values()
                if j == 7:
                    need(sc, divided, p.times(3) + (PAIRS + 3))
                    sigmoid(vT, gate).then_inc(g_sig, 1)

            def hg_last(p, j):
                if j == 0:
                    need(sc, level_done, p.times(LEVELS + 1) + (LEVELS + 1))
                    copy(att_cross, aux[:, 2, 0:2 * P].rearrange("p (h t) -> p h t", h=2)).then_inc(cross_att, 1)
                if j == 1:
                    need(sc, hg_pv, p + 1)
                    nc.scalar.activation(xl[0], aux[:, 0, :].rearrange("p (h t) -> p h t", h=2),
                                         ACT.Square).then_inc(hg_sq, 1)
                if j == 2:
                    need(sc, hg_mean, p + 1)
                    root(suf, aux[:, 3, :].rearrange("p (h t) -> p h t", h=2), 1.0 / P).then_inc(hg_rms, 1)
                if j == 3:
                    need(sc, hg_o, p + 1)
                    copy(mid[:, tiles_of(p), 0, :], xl[0]).then_inc(hg_hi, 1)

            for j in range(HG_SLOTS):
                hg_own(Count(0), j)
                sb_last(PAIRS - 1, j)
            with sc.Fori(1, PAIRS) as i:
                for j in range(HG_SLOTS):
                    hg_own(Count(0, 1, i), j)
                    hg_last(Count(-1, 1, i), j)

            def square(pair_no):
                nc.scalar.activation(sq, xT[:, both(pair_no), :], ACT.Square).then_inc(sq_ready, 1)

            def out_rows(m):
                sc.wait_ge(o_T, m + 1)
                copy(stage[:, :, m * COLS:(m + 1) * COLS],
                     aux[:, 1 + m % 2, :].rearrange("p (h d) -> p h d", h=2)).then_inc(o_copied, 1)

            def prepare(gain, pair_no):
                for c in range(2):
                    tile = pair_no + c
                    ins = nc.scalar.mul(act[:, one(tile), 0, :], xT[:, one(tile), :],
                                        vecs[:, one(tile + gain)])
                ins.then_inc(next_hi, 1)

            for j in range(8):
                split(Count(S_OUTB + j + RING))
                hg_last(Count(PAIRS - 1), j)
            for j in range(8):
                split(Count(S_OUTA + j + RING))
                sc.wait_ge(job_emptied, J_OUTA + j + 1)
                prepare(V_FFN, Count(2 * j))
                sc.wait_ge(sumsq, j + 1)
                square(Count(2 * j))

            def unit(s, job, u):
                split(s + RING)
                take_cross(s + 1, job)
                split(s + (RING + 1))
                need(sc, t_scaled, u + 1)
                sigmoid(sig, tgate).then_inc(t_sig, 1)
                split(s + (RING + 2))
                take_cross(s + 3, job + 1)
                split(s + (RING + 3))
                need(sc, u_made, u + 1)

            def first_unit(layer, s, job, u):
                if layer == 1:
                    mixed(GROUPS - 1)
                split(s + RING)
                split(s + (RING + 1))
                mean_root(layer)
                take_cross(s + 2, job)
                split(s + (RING + 2))
                need(sc, t_scaled, u + 1)
                sigmoid(sig, tgate).then_inc(t_sig, 1)
                take_cross(s + 3, job + 1)
                split(s + (RING + 3))
                need(sc, u_made, u + 1)

            def mixed(g):
                for n in (2 * g, 2 * g + 1):
                    sc.wait_ge(x_mixed, n + 1)
                    prepare(V_FFN + DT, Count(2 * n))
                    sc.wait_ge(sumsq, 9 * 2 + n + 1)
                    square(Count(2 * n))

            def hidden_hi(u_local):
                copy(mid[:, both(u_local), 0, :], tup).then_inc(g_hi, 1)

            def mean_root(layer):
                sc.wait_ge(mean_done, 2 * layer + 1)
                root(rstd[:], aux[:, 0, 0:TOKENS], 1.0 / D).then_inc(rms_done, 1)

            for layer, (s_ffn, j_ffn) in enumerate(((S_FFN0, J_FFN0), (S_FFN1, J_FFN1))):
                if layer == 1:
                    sc.wait_ge(mean_done, 2)
                    root(rows[:], aux[:, 3, 0:2], 1.0 / D).then_inc(row_rms, 1)
                    for g in range(GROUPS):
                        sc.wait_ge(slot_used, S_POOL + g + 1)
                        sc.wait_ge(row_rstd, 2)
                        need(sc, mix_done, g - 1)
                        nc.scalar.mul(zt[g % 2][:, 0, :], bank(Count(J_POOL + g))[:, 0, :], rows[:, 0:1]
                                      ).then_inc(z_kept, 1)
                        split(Count(S_POOL + g + RING))
                        if g > 0:
                            mixed(g - 1)
                for g, (s0, j0, u0, n) in enumerate(ffn_groups(s_ffn, j_ffn)):
                    first = 0
                    ub = sum(UNITS) * layer + u0
                    if g == 0:
                        first_unit(layer, Count(s0), Count(j0), Count(ub))
                        hidden_hi(Count(0))
                        first = 1
                    with sc.Fori(first, n) as i:
                        unit(Count(s0, 4, i), Count(j0, 2, i), Count(ub, 1, i))
                        hidden_hi(Count(0, 2, i))
                    s1, j1 = s0 + 4 * n, j0 + 2 * n
                    last = g == len(UNITS) - 1
                    if not last:
                        with sc.Fori(0, 4) as i:
                            for j in range(4):
                                split(Count(s1 + j + RING, 4, i))
                        continue
                    for j, (m, half) in enumerate(down_slots(8)):
                        if s1 + j + RING < SLOTS:
                            split(Count(s1 + j + RING))
                        if half == 0:
                            continue
                        sc.wait_ge(job_emptied, j1 + m + 1)
                        sc.wait_ge(sumsq, 9 * (2 * layer + 1) + m + 1)
                        square(Count(2 * m))
                        if layer == 0:
                            prepare(V_MIX + DT, Count(2 * m))
                        elif m > 0:
                            out_rows(m - 1)
                    if layer == 1:
                        out_rows(7)
            sc.wait_ge(mean_done, 4)
            root(rows[:], aux[:, 3, 0:2], 1.0 / D).then_inc(row_rms, 1)
            sc.wait_ge(row_rstd, 3)
            for c in range(2):
                nc.scalar.mul(stage[:, 1, c * 1024:(c + 1) * 1024], stage[:, 1, c * 1024:(c + 1) * 1024],
                              rows[:, 1:2]).then_inc(out_scaled[1], 1)

        @block.vector
        def _(ve):
            V = nc.vector
            chain = Chain(ve, dve_chain)

            def mul(out_, a, b):
                return V.tensor_tensor(out_, a, b, ALU.mult)

            def split(s):
                need(ve, hi_ready, s + 1)
                V.tensor_tensor(lo[:, s.place, :], raw[:, s.place, :], hi[:, s.place, :].bitcast(F32),
                                ALU.subtract).then_inc(lo_ready, 1)

            def empty(out_, s, job, crosses):
                need(ve, cross_ready, crosses + 1)
                V.tensor_tensor(out_, bank(job)[:, :, 0:TOKENS], cross[:], ALU.add).then_inc(job_emptied, 1)

            def divide(a, job):
                need(ve, job_emptied, job + 1)
                mul(a, a, rstd2).then_inc(divided, 1)

            def add_residual(s, job, pair_no):
                need(ve, slot_used, s + 1)
                xs = xT[:, both(pair_no), :]
                for half in range(2):
                    ps = bank(job)[:, :, half * TOKENS:(half + 1) * TOKENS]
                    ins = V.tensor_tensor(xs, xs, ps, ALU.add)
                    if half == 0:
                        chain.link(ins)
                        chain.settle()
                ins.then_inc(job_emptied, 1)

            def prepare(gain, prepared, pair_no):
                need(ve, next_hi, prepared + 1)
                for c in range(2):
                    tile = pair_no + c
                    ins = V.scalar_tensor_tensor(act[:, one(tile), 1, :], xT[:, one(tile), :],
                                                 vecs[:, one(tile + gain)],
                                                 act[:, one(tile), 0, :].bitcast(F32), ALU.mult, ALU.subtract)
                    if c == 0:
                        chain.link(ins)
                ins.then_inc(next_ready, 1)

            def h_lo(n):
                ve.wait_ge(h_hi, n + 1)
                for c in range(2):
                    ins = V.scalar_tensor_tensor(act[:, 2 * n + c, 1, :], start_bank(n)[:, c, :],
                                                 vecs[:, V_MIX + 2 * n + c:V_MIX + 2 * n + c + 1],
                                                 act[:, 2 * n + c, 0, :].bitcast(F32), ALU.mult, ALU.subtract)
                    if c == 0:
                        chain.link(ins)
                ins.then_inc(h_ready, 1)

            def copy_x(n):
                V.tensor_copy(xT[:, 2 * n:2 * n + 2, :], start_bank(n)).then_inc(x_copied, 1)

            for n in range(4):
                h_lo(n)
            copy_x(0)
            copy_x(1)
            split(Count(0))
            for n in range(4, 8):
                h_lo(n)
            copy_x(2)
            copy_x(3)
            split(Count(1))
            split(Count(2))
            for n in range(4, 8):
                copy_x(n)
            split(Count(3))
            V.tensor_tensor(lbs[:, 1, :], vecs[:, V_LB:V_LB + HEADS], vecs[:, V_LB + HEADS:V_LB + 2 * HEADS],
                            ALU.subtract).then_inc(lb_diff, 1)
            ve.wait_ge(row_rms, 1)
            V.reciprocal(rows[:], rows[:]).then_inc(row_rstd, 1)
            ve.wait_ge(row_rstd, 1)
            for h in range(2):
                V.tensor_scalar(diag[:, h, :], ident[:], rows[:, h:h + 1], None, ALU.mult).then_inc(diag_ready, 1)
            for n, sign in enumerate((1.0, -1.0)):
                V.tensor_scalar(z_scale[:, n, :], rows[:], sign * float(P) ** -0.5, None, ALU.mult
                                ).then_inc(z_scale_made, 1)

            def sb_last(p, j):
                if j == 1:
                    ve.wait_ge(sb_hi, p + 1)
                    V.tensor_tensor(mid[:, 8 + 2 * p:10 + 2 * p, 1, :],
                                    aux[:, 3, :].rearrange("p (h t) -> p h t", h=2),
                                    mid[:, 8 + 2 * p:10 + 2 * p, 0, :].bitcast(F32), ALU.subtract).then_inc(sb_out, 1)

            for p in range(PAIRS):
                for j in range(SB_SLOTS):
                    s, job = Count(SB_SLOTS * p + j), Count(SB_JOBS * p + j // 2)
                    if j == 1:
                        need(ve, z_done, p)
                        empty(q, s, job, job)
                    if j == 3:
                        if p == 0:
                            ve.wait_ge(rstd_bc, 1)
                            chain.link(V.tensor_copy(rstd[:], aux[:, 3, 0:TOKENS]))
                            ve.wait_ge(lb_ready, 1)
                            chain.link(V.tensor_scalar(lbs[:, 1, :], lbs[:, 0, :], -1.0, 1.0, ALU.mult, ALU.add))
                            chain.settle()
                        empty(k, s, job, job)
                        divide(k, job)
                    if j == 5:
                        need(ve, v_T, p)
                        empty(vT, s, job, job)
                    split(s + RING)
                    if j == 4:
                        ve.wait_ge(sb_sig, p + 1)
                        for at in (0, P + 1 + P):
                            a, b = kp2[:, :, at:at + P], sg2[:, :, at:at + P]
                            chain.link(V.tensor_tensor(a, a, tri[:, 1:2, :].to_broadcast((P, 2, P)), ALU.max))
                            chain.link(V.tensor_tensor(b, b, tri[:, 0:1, :].to_broadcast((P, 2, P)), ALU.mult))
                        chain.settle()
                        chain.link(V.tensor_tensor_scan(cum[:, ::-1], kp[:, ::-1], reset[:, ::-1], 0.0,
                                                        ALU.mult, ALU.add))
                        chain.settle()
                        mul(sg[:, 0:2 * W2 - 1], sg[:, 0:2 * W2 - 1], cum[:, 1:2 * W2]).then_inc(w_ready, 1)
                    if p > 0:
                        sb_last(p - 1, j)

            def halves(a, lv):
                return a.rearrange("p h (n two j) -> p (h n) two j", two=2, j=1 << lv)

            def level(p, lv):
                h, n = 1 << lv, TOKENS >> lv
                X, Q, K, A, B = (halves(a, lv) for a in (xl[lv % 2], q, k, pre, suf))
                need(ve, level_done, p.times(LEVELS + 1) + (lv - 1))
                chain.link(mul(X[:, :, 0, :], K[:, :, 0, :], B[:, :, 0, :]))
                if lv > 0:
                    chain.settle()
                mul(X[:, :, 1, :], Q[:, :, 1, :], A[:, :, 1, :]).then_inc(x_level, 1)
                if lv > 1:
                    keep_level(lv - 2)
                if lv < LEVELS:
                    chain.settle()
                    chain.link(mul(B[:, :, 0, :], B[:, :, 0, :], A[:, :, 1, h - 1:h].to_broadcast((P, n, h))))
                    chain.settle()
                    chain.link(mul(A[:, :, 1, :], A[:, :, 1, :], A[:, :, 0, h - 1:h].to_broadcast((P, n, h))))

            def keep_level(lv):
                h = 1 << lv
                o = att_own.rearrange("p g (n two j) -> p g n two j", two=2, j=h)[:, :, :, 1, :]
                m = lmask[:, lv:lv + 1, :].rearrange("p a (n j) -> p a n j", j=h).to_broadcast((P, 4, 64 // h, h))
                d = aux[:, 1 + lv % 2, 0:4 * 64].rearrange("p (g n j) -> p g n j", g=4, j=h)
                V.copy_predicated(o, m.bitcast(U32), d).then_inc(level_kept, 1)

            def hg_own(p, j):
                s, job = p.times(HG_SLOTS) + (S_HG + j), p.times(HG_JOBS) + (J_HG + j // 2)
                if j == 1:
                    need(ve, diag_done, p)
                    if p.stride == 0:
                        ve.wait_ge(w_T, PAIRS)
                    empty(k, s, job, job)
                    divide(k, job)
                    split(s + RING)
                    need(ve, f_sig, p + 1)
                    for c in range(2):
                        head = one(p.times(2) + c)
                        chain.link(V.tensor_scalar(pre[:, c, :], k[:, c, :], lbs[:, 1, head], lbs[:, 0, head],
                                                   ALU.mult, ALU.add))
                    chain.settle()
                    V.tensor_scalar(k, pre, -1.0, 1.0, ALU.mult, ALU.add).then_inc(f_ready, 1)
                elif j == 3:
                    empty(xl[1], s, job, job)
                    divide(xl[1], job)
                    split(s + RING)
                    chain.link(V.memset(suf, 1.0))
                    need(ve, q_sig, p + 1)
                    mul(q, q, xl[1]).then_inc(q_ready, 1)
                    need(ve, q_ready, p + 1)
                elif j == 5:
                    need(ve, diag_done, p + 1)
                    chain.link(mul(att_own, aux[:, 3, :].rearrange("p (g t) -> p g t", g=4),
                                   ident[:].unsqueeze(1).to_broadcast((P, 4, P))))
                    chain.settle()
                    level(p, 2)
                    need(ve, v_T, p + PAIRS)
                    empty(vT, s, job, job)
                    level(p, 3)
                    split(s + RING)
                elif j == 7:
                    level(p, 6)
                    level(p, 7)
                    empty(gate, s, job, job)
                    divide(gate, job)
                    split(s + RING)
                    need(ve, g_sig, p + 1)
                    mul(gate, gate, vT).then_inc(g_ready, 1)
                elif j == 4:
                    need(ve, f_ready, p + 1)
                    need(ve, hg_out, p)
                    chain.settle()
                    level(p, 0)
                    level(p, 1)
                    split(s + RING)
                elif j == 6:
                    level(p, 4)
                    level(p, 5)
                    split(s + RING)
                else:
                    split(s + RING)

            def hg_last(p, j):
                if j == 0:
                    keep_level(LEVELS - 1)
                if j == 2:
                    need(ve, hg_rms, p + 1)
                    need(ve, g_ready, p + 1)
                    chain.link(V.reciprocal(suf, suf))
                    chain.settle()
                    chain.link(mul(xl[0], aux[:, 0, :].rearrange("p (h t) -> p h t", h=2), suf))
                    chain.settle()
                    for c in range(2):
                        ins = V.scalar_tensor_tensor(xl[0][:, c, :], xl[0][:, c, :], vecs[:, V_HGN:V_HGN + 1],
                                                     gate[:, c, :], ALU.mult, ALU.mult)
                        if c == 0:
                            chain.link(ins)
                    ins.then_inc(hg_o, 1)
                if j == 3:
                    need(ve, hg_hi, p + 1)
                    V.tensor_tensor(mid[:, tiles_of(p), 1, :], xl[0], mid[:, tiles_of(p), 0, :].bitcast(F32),
                                    ALU.subtract).then_inc(hg_out, 1)

            for j in range(HG_SLOTS):
                hg_own(Count(0), j)
                sb_last(PAIRS - 1, j)
            with chain.loop(1, PAIRS, HG_LINKS) as i:
                for j in range(HG_SLOTS):
                    if j == 0:
                        need(ve, level_done, Count(LEVELS - (LEVELS + 1), LEVELS + 1, i))
                        need(ve, level_kept, Count(-1, LEVELS, i))
                    hg_own(Count(0, 1, i), j)
                    hg_last(Count(-1, 1, i), j)

            for j in range(8):
                if j == 0:
                    ve.wait_ge(level_done, (LEVELS + 1) * PAIRS - 1)
                    ve.wait_ge(level_kept, LEVELS * PAIRS - 1)
                add_residual(Count(S_OUTB + j), Count(J_OUTB + j), Count(2 * j))
                split(Count(S_OUTB + j + RING))
                hg_last(Count(PAIRS - 1), j)
            for j in range(8):
                add_residual(Count(S_OUTA + j), Count(J_OUTA + j), Count(2 * j))
                split(Count(S_OUTA + j + RING))
                prepare(V_FFN, Count(PREP_FFN0 + j), Count(2 * j))

            def unit(s, job, u, c, tile):
                split(s + RING)
                empty(tgate, s + 1, job, c)
                need(ve, job_emptied, job + 1)
                mul(tgate, tgate, rstd2).then_inc(t_scaled, 1)
                split(s + (RING + 1))
                need(ve, t_sig, u + 1)
                chain.link(mul(tgate, tgate, sig))
                split(s + (RING + 2))
                need(ve, hidden, u)
                empty(tup, s + 3, job + 1, c + 1)
                need(ve, job_emptied, job + 2)
                chain.link(mul(tup, tup, rstd2))
                chain.settle()
                mul(tup, tup, tgate).then_inc(u_made, 1)
                split(s + (RING + 3))
                need(ve, g_hi, u + 1)
                V.tensor_tensor(mid[:, both(tile), 1, :], tup, mid[:, both(tile), 0, :].bitcast(F32),
                                ALU.subtract).then_inc(hidden, 1)

            def first_unit(layer, s, job, u, c, tile):
                if layer == 1:
                    mix_in(GROUPS - 1)
                    prepare_group(GROUPS - 1)
                split(s + RING)
                split(s + (RING + 1))
                invert(layer)
                empty(tgate, s + 2, job, c)
                need(ve, job_emptied, job + 1)
                mul(tgate, tgate, rstd2).then_inc(t_scaled, 1)
                split(s + (RING + 2))
                need(ve, t_sig, u + 1)
                chain.link(mul(tgate, tgate, sig))
                need(ve, hidden, u)
                empty(tup, s + 3, job + 1, c + 1)
                need(ve, job_emptied, job + 2)
                chain.link(mul(tup, tup, rstd2))
                chain.settle()
                mul(tup, tup, tgate).then_inc(u_made, 1)
                split(s + (RING + 3))
                need(ve, g_hi, u + 1)
                V.tensor_tensor(mid[:, both(tile), 1, :], tup, mid[:, both(tile), 0, :].bitcast(F32),
                                ALU.subtract).then_inc(hidden, 1)

            def mix_in(g):
                ve.wait_ge(mix_done, g + 1)
                for d in range(4):
                    t = 4 * g + d
                    ins = V.scalar_tensor_tensor(xT[:, t, :],
                                                 aux[:, 2 * (g % 2) + d // 2, (d % 2) * TOKENS:(d % 2 + 1) * TOKENS],
                                                 vecs[:, V_SCALE + t:V_SCALE + t + 1], xT[:, t, :], ALU.mult, ALU.add)
                    if d % 2:
                        ins.then_inc(x_mixed, 1)

            def prepare_group(g):
                ve.wait_ge(x_mixed, 2 * g + 2)
                for n in (2 * g, 2 * g + 1):
                    prepare(V_FFN + DT, Count(PREP_FFN1 + n), Count(2 * n))

            def invert(layer):
                ve.wait_ge(rms_done, layer + 1)
                chain.link(V.reciprocal(rstd[:], rstd[:]))
                chain.settle()

            for layer, (s_ffn, j_ffn) in enumerate(((S_FFN0, J_FFN0), (S_FFN1, J_FFN1))):
                if layer == 1:
                    ve.wait_ge(row_rms, 2)
                    V.reciprocal(rows[:], rows[:]).then_inc(row_rstd, 1)
                    for g in range(GROUPS):
                        ve.wait_ge(slot_used, S_POOL + g + 1)
                        ve.wait_ge(row_rstd, 2)
                        need(ve, mix_done, g - 1)
                        V.tensor_scalar(zt[g % 2][:, 1, :], bank(Count(J_POOL + g))[:, 1, :], rows[:, 1:2], None,
                                        ALU.mult).then_inc(job_emptied, 1)
                        if g > 0:
                            mix_in(g - 1)
                        split(Count(S_POOL + g + RING))
                        if g > 0:
                            prepare_group(g - 1)
                for g, (s0, j0, u0, n) in enumerate(ffn_groups(s_ffn, j_ffn)):
                    first = 0
                    ub = sum(UNITS) * layer + u0
                    cb = C_FFN + 2 * ub
                    if g == 0:
                        first_unit(layer, Count(s0), Count(j0), Count(ub), Count(cb), Count(0))
                        first = 1
                    with chain.loop(first, n, 2) as i:
                        unit(Count(s0, 4, i), Count(j0, 2, i), Count(ub, 1, i), Count(cb, 2, i), Count(0, 2, i))
                    s1, j1 = s0 + 4 * n, j0 + 2 * n
                    if g < len(UNITS) - 1:
                        with chain.loop(0, 4, 2) as i:
                            for j, (m, half) in enumerate(down_slots(2)):
                                if half == 1:
                                    add_residual(Count(s1 + j, 4, i), Count(j1 + m, 2, i), Count(2 * m, 4, i))
                                split(Count(s1 + j + RING, 4, i))
                        continue
                    for j, (m, half) in enumerate(down_slots(8)):
                        if half == 1:
                            add_residual(Count(s1 + j), Count(j1 + m), Count(2 * m))
                        if half == 1 and layer == 1:
                            ve.wait_ge(job_emptied, j1 + m + 1)
                            need(ve, o_T, m - 1)
                            for c in range(2):
                                ins = V.tensor_scalar(xg[m % 2][:, c, :], xT[:, 2 * m + c, :],
                                                      vecs[:, V_FINAL + 2 * m + c:V_FINAL + 2 * m + c + 1], None,
                                                      ALU.mult)
                                if c == 0:
                                    chain.link(ins)
                            ins.then_inc(xg_ready, 1)
                        if s1 + j + RING < SLOTS:
                            split(Count(s1 + j + RING))
                        if half == 1 and layer == 0:
                            prepare(V_MIX + DT, Count(PREP_POOL + m), Count(2 * m))
            ve.wait_ge(row_rms, 3)
            V.reciprocal(rows[:], rows[:]).then_inc(row_rstd, 1)
            ve.wait_ge(row_rstd, 3)
            ve.wait_ge(o_copied, 8)
            for c in range(2):
                V.tensor_scalar(stage[:, 0, c * 1024:(c + 1) * 1024], stage[:, 0, c * 1024:(c + 1) * 1024],
                                rows[:, 0:1], None, ALU.mult).then_inc(out_scaled[0], 1)

        @block.tensor
        def _(pe):
            mm = nc.tensor.matmul

            def slot(s, job, rhs, k0, depth, first, last):
                if first:
                    need(pe, job_emptied, job + (-1))
                need(pe, lo_ready, s + 1)
                for c in range(2):
                    for n in range(depth):
                        at = n * COLS + c * P
                        mm(bank(job)[:, c, :], hi[:, s.place, at:at + P], rhs[:, k0 + n, :, :],
                           start=(first and n == 0), stop=False)
                        ins = mm(bank(job)[:, c, TOKENS:], lo[:, s.place, at:at + P], rhs[:, k0 + n, 0, :],
                                 start=False, stop=(last and n == depth - 1))
                ins.then_inc(slot_used, 1)

            def turn(out_, in_):
                return nc.tensor.transpose(out_, in_, ident[:])

            def turn_x(n, h):
                for c in range(2):
                    ins = turn(start_bank(n)[:, c, h * P:(h + 1) * P], stage[:, h, (2 * n + c) * P:(2 * n + c + 1) * P])
                return ins

            pe.wait_ge(ident_made, 1)
            pe.wait_ge(x_loaded[0], 16)
            for n in range(7):
                turn_x(n, 0)
            pe.wait_ge(vec_loaded, 6 * 16)
            nc.tensor.transpose(aux[:, 3, 0:V_ALL], vrows[0:V_ALL, :], ident[0:V_ALL, 0:V_ALL]).then_inc(vec_T, 1)
            pe.wait_ge(x_loaded[1], 16)
            for n in range(7):
                turn_x(n, 1).then_inc(x_T, 1)
            pe.wait_ge(vecs_ready, 1)
            turn_x(7, 0)
            turn_x(7, 1).then_inc(x_T, 1)

            def weigh(o, h, a00, a01, a11, **kw):
                mm(o[:, 0:P], vnat[:, h, 0, :], a00, start=True, stop=False)
                mm(o[:, P:2 * P], vnat[:, h, 0, :], a01, start=False, stop=False)
                return mm(o[:, P:2 * P], vnat[:, h, 1, :], a11, start=False, stop=True)

            def turn_v():
                for h in range(2):
                    for n in range(2):
                        ins = turn(aux[:, 0, (2 * h + n) * P:(2 * h + n + 1) * P], vT[:, h, n * P:(n + 1) * P])
                ins.then_inc(v_T, 1)

            def sb_last(p, j):
                if j == 0:
                    pe.wait_ge(w_ready, p + 1)
                    for h in range(2):
                        for n, at in enumerate((0, P + 1, 2 * P + 1)):
                            ins = turn(aux[:, 1 + h, n * P:(n + 1) * P], sg2[:, h, at:at + P])
                    ins.then_inc(w_T, 1)
                    pe.wait_ge(job_emptied, SB_JOBS * p + 3)
                    turn_v()
                if j == 1:
                    pe.wait_ge(wt_ready, p + 1)
                    pe.wait_ge(vnat_ready, p + 1)
                    need(pe, sb_out, p)
                    for h in range(2):
                        ins = weigh(aux[:, 3, h * TOKENS:(h + 1) * TOKENS], h, *(att[:, h, n, :] for n in range(3)))
                    ins.then_inc(sb_pv, 1)

            for p in range(PAIRS):
                for j in range(SB_SLOTS):
                    if p == 0 and j < 2:
                        pe.wait_ge(h_ready, 4 * (j + 1))
                    if p == 0 and j in (0, 2):
                        pe.wait_ge(x_copied, 2 + j)
                    slot(Count(SB_SLOTS * p + j), Count(SB_JOBS * p + j // 2), act, DEPTH * (j % 2), DEPTH,
                         j % 2 == 0, j % 2 == 1)
                    if p == 0 and j == 2:
                        pe.wait_ge(diag_ready, 2)
                        pe.wait_ge(x_copied, 8)
                        mm(aux[:, 3, 0:TOKENS], ones[:], diag.rearrange("p h t -> p (h t)"), start=True, stop=True
                           ).then_inc(rstd_bc, 1)
                    if j == 4:
                        pe.wait_ge(divided, p + 1)
                        for h in range(2):
                            mm(aux[:, 1 + h, 0:P], q[:, h, 0:P], k[:, h, 0:P], start=True, stop=True)
                            ins = mm(aux[:, 1 + h, P:3 * P], q[:, h, P:], k[:, h, :], start=True, stop=True)
                        ins.then_inc(z_done, 1)
                    if p > 0:
                        sb_last(p - 1, j)

            def level(p, lv):
                need(pe, x_level, p.times(LEVELS + 1) + (lv + 1))
                need(pe, level_kept, p.times(LEVELS) + (lv - 1 if lv else 0))
                if lv == 1:
                    need(pe, cross_att, p)
                X = xl[lv % 2]
                for h in range(2):
                    if lv == LEVELS:
                        ins = mm(aux[:, 2, h * P:(h + 1) * P], X[:, h, 0:P], X[:, h, P:], start=True, stop=True)
                        continue
                    for n in range(2):
                        tile = X[:, h, n * P:(n + 1) * P]
                        upper = tile.rearrange("p (n two j) -> p n two j", two=2, j=1 << lv)[:, :, 1, :]
                        ins = mm(aux[:, 1 + lv % 2, (2 * h + n) * 64:(2 * h + n + 1) * 64], tile, upper,
                                 start=True, stop=True)
                ins.then_inc(level_done, 1)

            def hg_own(p, j):
                s, job = p.times(HG_SLOTS) + (S_HG + j), p.times(HG_JOBS) + (J_HG + j // 2)
                slot(s, job, act, DEPTH * (j % 2), DEPTH, j % 2 == 0, j % 2 == 1)
                if j == 5:
                    need(pe, q_ready, p + 1)
                    need(pe, hg_rms, p)
                    for h in range(2):
                        for n in range(2):
                            ins = mm(aux[:, 3, (2 * h + n) * P:(2 * h + n + 1) * P], k[:, h, n * P:(n + 1) * P],
                                     q[:, h, n * P:(n + 1) * P], start=True, stop=True)
                    ins.then_inc(diag_done, 1)
                    level(p, 0)
                    level(p, 1)
                if j == 6:
                    need(pe, job_emptied, p.times(HG_JOBS) + (J_HG + 3))
                    need(pe, hg_o, p)
                    turn_v()
                    level(p, 2)
                    level(p, 3)
                if j == 7:
                    level(p, 4)
                    level(p, 5)

            def hg_last(p, j):
                if j == 0:
                    level(p, 6)
                    level(p, 7)
                if j == 1:
                    need(pe, level_kept, p.times(LEVELS) + LEVELS)
                    need(pe, cross_att, p + 1)
                    need(pe, vnat_ready, p + (PAIRS + 1))
                    for h in range(2):
                        ins = weigh(aux[:, 0, h * TOKENS:(h + 1) * TOKENS], h,
                                    att_own[:, 2 * h, :], att_cross[:, h, :], att_own[:, 2 * h + 1, :])
                    ins.then_inc(hg_pv, 1)
                if j == 2:
                    need(pe, hg_sq, p + 1)
                    mm(aux[:, 3, :], ones[:], xl[0].rearrange("p h t -> p (h t)"), start=True, stop=True
                       ).then_inc(hg_mean, 1)

            for j in range(HG_SLOTS):
                hg_own(Count(0), j)
                sb_last(PAIRS - 1, j)
            with pe.Fori(1, PAIRS) as i:
                for j in range(HG_SLOTS):
                    hg_own(Count(0, 1, i), j)
                    hg_last(Count(-1, 1, i), j)
            pe.wait_ge(sb_out, PAIRS)
            for j in range(8):
                slot(Count(S_OUTB + j), Count(J_OUTB + j), mid, 8, DEPTH, True, True)
                hg_last(Count(PAIRS - 1), j)
            pe.wait_ge(hg_out, PAIRS)
            for j in range(8):
                slot(Count(S_OUTA + j), Count(J_OUTA + j), mid, 0, DEPTH, True, True)

            def mean(n):
                pe.wait_ge(sumsq, 9 * (n + 1))
                for c in range(2):
                    ins = mm(aux[:, 0, 0:TOKENS], ones[:], acc[:, c, :], start=(c == 0), stop=(c == 1))
                ins.then_inc(mean_done, 1)

            def row_mean(n):
                pe.wait_ge(sumsq, 9 * (n + 1))
                for h in range(2):
                    for c in range(2):
                        ins = mm(aux[:, 3, h:h + 1], acc[:, c, h * P:(h + 1) * P], ones[:, 0:1],
                                 start=(c == 0), stop=(c == 1))
                ins.then_inc(mean_done, 1)

            def pool_slot(g):
                s, job = Count(S_POOL + g), Count(J_POOL + g)
                pe.wait_ge(next_ready, PREP_POOL + 2 * g + 2)
                need(pe, job_emptied, job + (-1))
                need(pe, lo_ready, s + 1)
                for h in range(2):
                    for n in range(4):
                        tile = act[:, 4 * g + n, :, h * P:(h + 1) * P]
                        w_hi, w_lo = (a[:, s.place, n * 512:(n + 1) * 512] for a in (hi, lo))
                        mm(bank(job)[:, h, :], tile[:, 0, :], w_hi, start=(n == 0), stop=False)
                        mm(bank(job)[:, h, :], tile[:, 0, :], w_lo, start=False, stop=False)
                        ins = mm(bank(job)[:, h, :], tile[:, 1, :], w_hi, start=False, stop=(n == 3))
                ins.then_inc(slot_used, 1)

            def mix(g):
                if g == 0:
                    pe.wait_ge(windows_made, 2 * GROUPS)
                pe.wait_ge(z_kept, g + 1)
                pe.wait_ge(job_emptied, J_POOL + g + 1)
                need(pe, x_mixed, 2 * (g - 1))
                Z = zt[g % 2]
                for d in range(4):
                    at = (d % 2) * TOKENS
                    o = aux[:, 2 * (g % 2) + d // 2, at:at + TOKENS]
                    z0, z1 = (Z[:, h, d * P:(d + 1) * P] for h in range(2))
                    mm(o[:, 0:P], z0, window[:, g, 0:P], start=True, stop=False)
                    mm(o[:, P:], z1, window[:, g, P + SPILL:], start=False, stop=False)
                    ins = mm(o[:, P:P + SPILL], z0, window[:, g, P:P + SPILL], start=False, stop=True)
                ins.then_inc(mix_done, 1)

            for layer, (s_ffn, j_ffn) in enumerate(((S_FFN0, J_FFN0), (S_FFN1, J_FFN1))):
                if layer == 1:
                    for g in range(GROUPS):
                        pool_slot(g)
                        if g == 0:
                            row_mean(1)
                        else:
                            mix(g - 1)
                for g, (s0, j0, u0, n) in enumerate(ffn_groups(s_ffn, j_ffn)):
                    first = 0
                    if g == 0:
                        for j in range(4):
                            if j % 2 == 0:
                                pe.wait_ge(next_ready, PREP_FFN1 * layer + 4 * (j // 2 + 1))
                            slot(Count(s0 + j), Count(j0 + j % 2), act, DEPTH * (j // 2), DEPTH, j < 2, j >= 2)
                            if layer == 1 and j == 0:
                                mix(GROUPS - 1)
                            if j == 1 + layer:
                                mean(2 * layer)
                        first = 1
                    with pe.Fori(first, n) as i:
                        for j in range(4):
                            slot(Count(s0 + j, 4, i), Count(j0 + j // 2, 2, i), act, DEPTH * (j % 2), DEPTH,
                                 j % 2 == 0, j % 2 == 1)
                    s1, j1 = s0 + 4 * n, j0 + 2 * n
                    done = sum(UNITS) * layer + u0
                    pe.wait_ge(hidden, done + n // 2)
                    if g < len(UNITS) - 1:
                        with pe.Fori(0, 4) as i:
                            for j, (m, half) in enumerate(down_slots(2)):
                                if j == 2:
                                    pe.wait_ge(hidden, done + n)
                                slot(Count(s1 + j, 4, i), Count(j1 + m, 2, i), mid, n * half, n, half == 0, half == 1)
                        continue

                    def turn_rows(m):
                        pe.wait_ge(xg_ready, m + 1)
                        need(pe, o_copied, m - 1)
                        for h in range(2):
                            for c in range(2):
                                ins = turn(aux[:, 1 + m % 2, h * TOKENS + c * P:h * TOKENS + (c + 1) * P],
                                           xg[m % 2][:, c, h * P:(h + 1) * P])
                        ins.then_inc(o_T, 1)

                    ended = None
                    for j, (m, half) in enumerate(down_slots(8)):
                        if j == 2:
                            pe.wait_ge(hidden, done + n)
                        slot(Count(s1 + j), Count(j1 + m), mid, n * half, n, half == 0, half == 1)
                        if layer == 1 and ended is not None:
                            turn_rows(ended)
                        ended = m if half else None
                if layer == 1:
                    turn_rows(7)
                    row_mean(3)


_INS = ["x", "mix_norm", "ffn_norm", "final_norm", "ab_w_in", "lb_logits", "hg_out_norm", "ab_w_out",
        "pool_w", "pool_scale", "ffn_w_gate", "ffn_w_up", "ffn_w_down"]


def kernel(**inputs):
    import numpy as np
    from concourse import bacc
    from concourse.bass_utils import run_bass_kernel_spmd

    nc = bacc.Bacc("TRN2", target_bir_lowering=False, num_devices=1)
    arrays, args = {}, []
    for name in _INS:
        a = np.ascontiguousarray(inputs[name])
        arrays[f"in_{name}"] = a
        args.append(nc.dram_tensor(f"in_{name}", a.shape, mybir.dt.from_np(a.dtype), kind="ExternalInput").ap())
    args.append(nc.dram_tensor("out_0", (1, TOKENS, D), F32, kind="ExternalOutput").ap())
    trunk(nc, *args)
    return run_bass_kernel_spmd(nc, [arrays], core_ids=[0]).results[0]["out_0"]
```
